# Optimizing a Trainium2 kernel written in Bass

```python
import numpy as np
import jax
import jax.numpy as jnp
from jax import lax

D_MODEL = 1024
BATCH = 1
SEQ = 512
DEPTH = 2

D_MIX = D_MODEL
HEAD_DIM = 64
H_FOX = 6
FOX_W = H_FOX * HEAD_DIM
CONV_GROUPS = 4
CONV_W = CONV_GROUPS * HEAD_DIM
CONV_K = 3
H_MLA = 6
Q_LORA = 256
KV_LORA = 256
QK_NOPE = 64
QK_ROPE = 32
V_DIM = 64
MLA_W = H_MLA * V_DIM
N_OUT_HEADS = D_MIX // HEAD_DIM
IN_W = 3 * FOX_W + H_FOX + 3 * CONV_W + Q_LORA + KV_LORA + QK_ROPE
ROPE_THETA = 10000.0
Q_BLOCK = 128
D_FF = 2816
N_EXPERTS = 8
TOP_K = 2
D_EXPERT = 3584
MOE_BLOCK = 128
N_DENSE = (DEPTH + 1) // 2
N_MOE = DEPTH // 2
ALPHA = (2 * DEPTH) ** 0.25
BETA = (8 * DEPTH) ** -0.25
LN_EPS = 1e-5
RMS_EPS = 1e-6

kernel_name = 'hybrid_fox_conv_mla_deepnorm_moe'

def _layer_norm(x, g, b):
    xf = x.astype(jnp.float32)
    xc = xf - jnp.mean(xf, axis=-1, keepdims=True)
    var = jnp.mean(xc * xc, axis=-1, keepdims=True)
    return (xc * lax.rsqrt(var + LN_EPS) * g + b).astype(x.dtype)

def _rms_norm(x, g):
    xf = x.astype(jnp.float32)
    return (xf * lax.rsqrt(jnp.mean(xf * xf, axis=-1, keepdims=True) + RMS_EPS) * g).astype(x.dtype)

def _rope(x, cos, sin):
    xf = x.astype(jnp.float32)
    x1, x2 = jnp.split(xf, 2, axis=-1)
    return jnp.concatenate([x1 * cos - x2 * sin, x2 * cos + x1 * sin], axis=-1).astype(x.dtype)

def _block_causal_attention(q, k, v, log_decay=None):
    bsz, seq, nh, dk = q.shape
    nblk = seq // Q_BLOCK
    scale = dk ** -0.5
    key_pos = jnp.arange(seq)
    q_blocks = q.reshape(bsz, nblk, Q_BLOCK, nh, dk).transpose(1, 0, 2, 3, 4)
    xs = (q_blocks, jnp.arange(nblk))
    if log_decay is not None:
        fk = log_decay.transpose(0, 2, 1)
        xs = xs + (log_decay.reshape(bsz, nblk, Q_BLOCK, nh).transpose(1, 0, 2, 3),)

    def one_block(blk):
        qb, i = blk[0], blk[1]
        s = jnp.einsum('bqhd,bkhd->bhqk', qb, k, preferred_element_type=jnp.float32) * scale
        if log_decay is not None:
            s = s + blk[2].transpose(0, 2, 1)[..., None] - fk[:, :, None, :]
        q_pos = i * Q_BLOCK + jnp.arange(Q_BLOCK)
        s = jnp.where(key_pos[None, :] <= q_pos[:, None], s, -jnp.inf)
        p = jax.nn.softmax(s, axis=-1)
        return jnp.einsum('bhqk,bkhd->bqhd', p.astype(v.dtype), v)

    out = lax.map(one_block, xs)
    return out.transpose(1, 0, 2, 3, 4).reshape(bsz, seq, nh, v.shape[-1])

def _causal_depthwise_conv(u, w):
    return lax.conv_general_dilated(
        u, w[:, None, :], window_strides=(1,), padding=[(CONV_K - 1, 0)],
        dimension_numbers=('NWC', 'WIO', 'NWC'), feature_group_count=u.shape[-1])

def _hybrid_mixer(h, w_in, b_f, w_conv, q_g, kv_g, w_uq, w_ukv, head_g, w_o, cos, sin):
    bsz, seq, _ = h.shape
    z = h @ w_in
    sizes = [FOX_W, FOX_W, FOX_W, H_FOX, CONV_W, CONV_W, CONV_W, Q_LORA, KV_LORA, QK_ROPE]
    (fq, fk, fv, f_logit, b_gate, c_gate, h_in, c_q, c_kv, k_rope) = jnp.split(
        z, np.cumsum(sizes)[:-1].tolist(), axis=-1)

    log_f = jax.nn.log_sigmoid(f_logit.astype(jnp.float32) + b_f.astype(jnp.float32))
    cum_log_f = jnp.cumsum(log_f, axis=1)
    o_fox = _block_causal_attention(
        fq.reshape(bsz, seq, H_FOX, HEAD_DIM), fk.reshape(bsz, seq, H_FOX, HEAD_DIM),
        fv.reshape(bsz, seq, H_FOX, HEAD_DIM), cum_log_f)

    o_conv = b_gate * _causal_depthwise_conv(c_gate * h_in, w_conv)

    q = (_rms_norm(c_q, q_g) @ w_uq).reshape(bsz, seq, H_MLA, QK_NOPE + QK_ROPE)
    q = jnp.concatenate([q[..., :QK_NOPE], _rope(q[..., QK_NOPE:], cos[:, None, :], sin[:, None, :])], axis=-1)
    kv = (_rms_norm(c_kv, kv_g) @ w_ukv).reshape(bsz, seq, H_MLA, QK_NOPE + V_DIM)
    k_r = _rope(k_rope, cos, sin)
    k = jnp.concatenate(
        [kv[..., :QK_NOPE], jnp.broadcast_to(k_r[:, :, None, :], (bsz, seq, H_MLA, QK_ROPE))], axis=-1)
    o_mla = _block_causal_attention(q, k, kv[..., QK_NOPE:])

    o = jnp.concatenate(
        [o_fox.reshape(bsz, seq, FOX_W), o_conv, o_mla.reshape(bsz, seq, MLA_W)], axis=-1)
    o = _rms_norm(o.reshape(bsz, seq, N_OUT_HEADS, HEAD_DIM), head_g.reshape(N_OUT_HEADS, HEAD_DIM))
    return o.reshape(bsz, seq, D_MIX) @ w_o

def _swiglu(x, wg, wu, wd):
    return (jax.nn.silu(x @ wg) * (x @ wu)) @ wd

def _moe_swiglu(h, w_router, wg, wu, wd):
    bsz, seq, dm = h.shape
    n_tok = bsz * seq
    xf = h.reshape(n_tok, dm)
    logits = (xf @ w_router).astype(jnp.float32)
    top_logits, top_idx = lax.top_k(logits, TOP_K)
    top_w = jax.nn.softmax(top_logits, axis=-1)
    n_asg = n_tok * TOP_K
    e_flat = top_idx.reshape(n_asg)
    tok_flat = jnp.arange(n_asg) // TOP_K
    order = jnp.argsort(e_flat)
    sorted_e = e_flat[order]
    counts = jnp.bincount(e_flat, length=N_EXPERTS)
    padded = (counts + MOE_BLOCK - 1) // MOE_BLOCK * MOE_BLOCK
    pad_end = jnp.cumsum(padded)
    pad_start = pad_end - padded
    start = jnp.cumsum(counts) - counts
    dest_sorted = pad_start[sorted_e] + (jnp.arange(n_asg) - start[sorted_e])
    n_blocks = -(-n_asg // MOE_BLOCK) + N_EXPERTS
    n_rows = n_blocks * MOE_BLOCK
    row_tok = jnp.full((n_rows,), n_tok, dtype=jnp.int32).at[dest_sorted].set(tok_flat[order].astype(jnp.int32))
    x_rows = jnp.concatenate([xf, jnp.zeros((1, dm), xf.dtype)], axis=0)[row_tok]
    block_e = jnp.minimum(
        jnp.searchsorted(pad_end, jnp.arange(n_blocks) * MOE_BLOCK, side='right'), N_EXPERTS - 1)

    def expert_block(args):
        xb, e = args
        return _swiglu(xb, wg[e], wu[e], wd[e])

    y_rows = lax.map(expert_block, (x_rows.reshape(n_blocks, MOE_BLOCK, dm), block_e)).reshape(n_rows, dm)
    dest = jnp.zeros((n_asg,), dtype=dest_sorted.dtype).at[order].set(dest_sorted)
    y = y_rows[dest].reshape(n_tok, TOP_K, dm)
    out = jnp.einsum('tk,tkd->td', top_w.astype(y.dtype), y)
    return out.reshape(bsz, seq, dm)

def setup_inputs(seed: int = 0) -> dict:
    key = jax.random.key(seed)
    ks = jax.random.split(key, 24)

    def nrm(k, shape, scale):
        return jax.random.normal(k, shape, jnp.float32) * scale

    return {
        'x': nrm(ks[0], (BATCH, SEQ, D_MODEL), 1.0),
        'c': nrm(ks[1], (BATCH, D_MODEL), 1.0),
        'w_mod': nrm(ks[2], (DEPTH, D_MODEL, 6 * D_MODEL), 0.3 * D_MODEL ** -0.5),
        'b_mod': nrm(ks[3], (DEPTH, 6 * D_MODEL), 0.02),
        'w_in': nrm(ks[4], (DEPTH, D_MODEL, IN_W), D_MODEL ** -0.5),
        'b_fgate': jnp.linspace(1.0, 5.0, H_FOX, dtype=jnp.float32)[None, :] + nrm(ks[5], (DEPTH, H_FOX), 0.1),
        'w_conv': nrm(ks[6], (DEPTH, CONV_K, CONV_W), CONV_K ** -0.5),
        'q_norm_g': 1.0 + nrm(ks[7], (DEPTH, Q_LORA), 0.02),
        'kv_norm_g': 1.0 + nrm(ks[8], (DEPTH, KV_LORA), 0.02),
        'w_uq': nrm(ks[9], (DEPTH, Q_LORA, H_MLA * (QK_NOPE + QK_ROPE)), Q_LORA ** -0.5),
        'w_ukv': nrm(ks[10], (DEPTH, KV_LORA, H_MLA * (QK_NOPE + V_DIM)), KV_LORA ** -0.5),
        'head_norm_g': 1.0 + nrm(ks[11], (DEPTH, D_MIX), 0.02),
        'w_o': nrm(ks[12], (DEPTH, D_MIX, D_MODEL), BETA * D_MIX ** -0.5),
        'ln1_g': 1.0 + nrm(ks[13], (DEPTH, D_MODEL), 0.02),
        'ln1_b': nrm(ks[14], (DEPTH, D_MODEL), 0.02),
        'ln2_g': 1.0 + nrm(ks[15], (DEPTH, D_MODEL), 0.02),
        'ln2_b': nrm(ks[16], (DEPTH, D_MODEL), 0.02),
        'ffn_w_gate': nrm(ks[17], (N_DENSE, D_MODEL, D_FF), D_MODEL ** -0.5),
        'ffn_w_up': nrm(ks[18], (N_DENSE, D_MODEL, D_FF), D_MODEL ** -0.5),
        'ffn_w_down': nrm(ks[19], (N_DENSE, D_FF, D_MODEL), BETA * D_FF ** -0.5),
        'router_w': nrm(ks[20], (N_MOE, D_MODEL, N_EXPERTS), D_MODEL ** -0.5),
        'exp_w_gate': nrm(ks[21], (N_MOE, N_EXPERTS, D_MODEL, D_EXPERT), D_MODEL ** -0.5),
        'exp_w_up': nrm(ks[22], (N_MOE, N_EXPERTS, D_MODEL, D_EXPERT), D_MODEL ** -0.5),
        'exp_w_down': nrm(ks[23], (N_MOE, N_EXPERTS, D_EXPERT, D_MODEL), BETA * D_EXPERT ** -0.5),
    }

def reference(x, c, w_mod, b_mod, w_in, b_fgate, w_conv, q_norm_g, kv_norm_g, w_uq, w_ukv,
              head_norm_g, w_o, ln1_g, ln1_b, ln2_g, ln2_b, ffn_w_gate, ffn_w_up, ffn_w_down,
              router_w, exp_w_gate, exp_w_up, exp_w_down):
    seq = x.shape[1]
    pos = jnp.arange(seq, dtype=jnp.float32)
    inv_freq = ROPE_THETA ** (-jnp.arange(0, QK_ROPE, 2, dtype=jnp.float32) / QK_ROPE)
    ang = pos[:, None] * inv_freq[None, :]
    cos, sin = jnp.cos(ang), jnp.sin(ang)
    c_act = jax.nn.silu(c)
    for layer in range(DEPTH):
        mod = c_act @ w_mod[layer] + b_mod[layer]
        shift1, scale1, gate1, shift2, scale2, gate2 = [m[:, None, :] for m in jnp.split(mod, 6, axis=-1)]
        h = x * (1.0 + scale1) + shift1
        y = _hybrid_mixer(h, w_in[layer], b_fgate[layer], w_conv[layer], q_norm_g[layer],
                          kv_norm_g[layer], w_uq[layer], w_ukv[layer], head_norm_g[layer],
                          w_o[layer], cos, sin)
        x = _layer_norm(ALPHA * x + (1.0 + gate1) * y, ln1_g[layer], ln1_b[layer])
        h = x * (1.0 + scale2) + shift2
        j = layer // 2
        if layer % 2 == 0:
            y = _swiglu(h, ffn_w_gate[j], ffn_w_up[j], ffn_w_down[j])
        else:
            y = _moe_swiglu(h, router_w[j], exp_w_gate[j], exp_w_up[j], exp_w_down[j])
        x = _layer_norm(ALPHA * x + (1.0 + gate2) * y, ln2_g[layer], ln2_b[layer])
    return x


_drawn_inputs = setup_inputs


def setup_inputs(seed=0):
    import zlib

    import numpy as np

    out = dict(_drawn_inputs(seed))
    spreads = {}
    factors = {'q_norm_g': 8.0, 'kv_norm_g': 5.372, 'head_norm_g': 4.138}
    for name, (base, spread) in spreads.items():
        noise = np.random.default_rng([zlib.crc32(name.encode()), seed]).standard_normal(out[name].shape)
        drawn = base * np.exp(spread * noise) if base else spread * noise
        out[name] = jnp.asarray(drawn.astype(out[name].dtype))
    for name, factor in factors.items():
        out[name] = (out[name] * factor).astype(out[name].dtype)
    return out
```

```python
import concourse.bass as bass
from concourse import mybir
from contextlib import ExitStack

P = 128
T, D = 512, 1024
TC, DC = T // P, D // P
NL = 2
HEADS, HD = 6, 64
KQ_MLA = 96
ROPE = 32
IN_W = 2470
FF, FE, NE = 2816, 3584, 8
EPS_LN, EPS_RMS = 1e-5, 1e-6
ALPHA = (2 * NL) ** 0.25
BIG = 1e30
Z0 = 3 * HEADS * HD
ZF, ZB, ZC, ZH, ZQ, ZK, ZR_ = 0, 6, 262, 518, 774, 1030, 1286
ZW = IN_W - Z0
C_ID, C_ONE, C_TRI, C_STRI, C_MASK, C_COS, C_SIN, C_IOTA, C_REV, C_ROW, C_EPS = (
    0, 128, 256, 384, 512, 640, 704, 768, 1280, 1288, 1296)
C_W = 1300
RING = 6
UNIT = 1024
PER_LAYER = 20 + 4 + 8
FFN_G, EXP_G = FF // 256, FE // 256
BASE = [0, PER_LAYER + 6 * FFN_G]
SWI_BASE = [PER_LAYER, BASE[1] + PER_LAYER]
WIDTHS = [P, 192, 256, 320, 384, 448, 512]
O_CHUNKS = [slice(0, 2), slice(2, 6, 3), slice(6, 8), slice(3, 5)]
O_ORDER = [0, 1, 2, 5, 6, 7, 3, 4]


def program(nc, a, out, ybuf):
    fp32, f32r, i32, u32 = mybir.dt.float32, mybir.dt.float32r, mybir.dt.int32, mybir.dt.uint32
    ACT, ALU, AX = mybir.ActivationFunctionType, mybir.AluOpType, mybir.AxisListType
    ds = bass.ds
    MUL, ADD, SUB, MAX, MIN = ALU.mult, ALU.add, ALU.subtract, ALU.max, ALU.min
    ctx = ExitStack()
    with ctx:
        start = (nc.sbuf_base + 31) // 32 * 32
        used = [start]

        def at(name, shape, dt, offset=None):
            size = 4
            for n in shape[1:]:
                size *= n
            if offset is None:
                offset = used[0]
                used[0] += (size + 31) // 32 * 32
            return nc.alloc_sbuf_tensor_at(name, shape, dt, offset=offset)

        sems = {}

        def sem(name):
            if name not in sems:
                sems[name] = ctx.enter_context(nc.semaphore(name))
            return sems[name]

        X = at("X", [P, TC, D], fp32)
        XL = at("XL", [P, TC, D], f32r, start)
        HTH = at("HTH", [P, DC, T], f32r)
        hth_at = start + 16384
        HTL = at("HTL", [P, DC, T], f32r)
        htl_at = hth_at + 16384
        RAW = [at(f"RAW{i}", [P, UNIT], fp32) for i in range(RING)]
        WH = [at(f"WH{i}", [P, UNIT], f32r) for i in range(RING)]
        WL = [at(f"WL{i}", [P, UNIT], f32r) for i in range(RING)]
        CST = at("CST", [P, C_W], fp32)
        TMP = at("TMP", [P, 2, T], fp32)
        GB = at("GB", [P, 2, D], fp32)
        ident = CST[:, C_ID:C_ID + P]
        ones = CST[:, C_ONE:C_ONE + P]
        VROW = at("VROW", [32, P], fp32)
        CACT = at("CACT", [P, DC], fp32)
        VCOL = at("VCOL", [P, 24], fp32)
        MODC = at("MODC", [P, 2 * NL * 2, DC], fp32)
        BF = at("BF", [P, NL, HEADS], fp32)
        FG = at("FG", [P, 4, TC * HEADS], fp32)
        SS = at("SS", [P, 2, 64], fp32)
        KRO = at("KRO", [P, TC, ROPE], fp32)
        RTK = at("RTK", [P, 4, 64], fp32)
        NM = at("NM", [P, 2, TC], fp32)
        RSUM = at("RSUM", [P, 2, TC], fp32)
        RD = at("RD", [P, 2, TC], fp32)
        BNS = at("BNS", [P, 2, 12], fp32)
        MV = at("MV", [P, 2, 2], fp32)
        LNS = at("LNS", [P, 2, 2], fp32)
        RW = at("RW", [P, DC, NE], fp32)
        RWH = at("RWH", [P, DC, NE], f32r)
        RWL = at("RWL", [P, DC, NE], f32r)
        RT8 = at("RT8", [P, 10, TC * NE], fp32)
        RT1 = at("RT1", [P, 8, TC], fp32)
        CNT = at("CNT", [P, NE], i32)
        ROWI = at("ROWI", [P, 2, TC], u32)
        ZERO = at("ZERO", [P, 512], f32r)
        arena = used[0]
        QA = at("QA", [P, HEADS, TC, KQ_MLA], fp32)
        KA = at("KA", [P, HEADS, TC, KQ_MLA], fp32)
        VA = at("VA", [P, HEADS, TC, HD], fp32)
        zr_at = used[0]
        ZR = at("ZR", [P, TC, ZW], fp32)
        oa_at = used[0]
        OA = at("OA", [P, TC, 16, HD], fp32)
        assert used[0] <= nc.sbuf_usable_end, (used[0], nc.sbuf_usable_end)
        MACC = [at(f"MACC{i}", [P, D], fp32, oa_at + 4096 * i) for i in range(2)]
        MODW = [at(f"MODW{i}", [P, D], fp32, oa_at + 4096 * (2 + i)) for i in range(2)]
        CN = at("CN", [P, TC, 512], fp32, htl_at + 8192)
        U1 = at("U1", [P, TC, 256], fp32, hth_at + 8192)
        U2 = at("U2", [P, TC, 256], fp32, hth_at + 12288)
        QT = [at(f"QT{i}", [P, T], fp32, hth_at + 8192 + 2048 * i) for i in range(2)]
        KT = [at(f"KT{i}", [P, T], fp32, hth_at + 12288 + 2048 * i) for i in range(2)]
        SQ = [at(f"SQ{i}", [P, TC, KQ_MLA], fp32, zr_at + 3072 * i) for i in range(2)]
        SK = [at(f"SK{i}", [P, TC, KQ_MLA], fp32, zr_at + 3072 * i + 1536) for i in range(2)]
        PR = [at(f"PR{i}", [P, T], fp32, zr_at + 6144 + 2048 * i) for i in range(2)]
        PTS = [at(f"PTS{i}", [P, T], fp32, zr_at + 10240 + 2048 * i) for i in range(2)]
        RTMP = at("RTMP", [P, 4, HEADS * TC * 16], fp32, zr_at + 14336)
        WCV = at("WCV", [P, 3, 256], fp32, oa_at + 8192)
        OSQ = at("OSQ", [P, TC, D], fp32, arena)
        ACC = at("ACC", [P, DC, T], fp32, arena)
        HAH = at("HAH", [P, 2, T], f32r, arena + 16384)
        HAL = at("HAL", [P, 2, T], f32r, arena + 20480)
        SIL = at("SIL", [P, 2, T], fp32, arena + 24576)
        LT = [at(f"LT{i}", [P, D], fp32, arena + 16384 + 4096 * i) for i in range(2)]
        LNR = at("LNR", [P, 2, D], fp32, arena + 24576)
        SEL = at("SEL", [P, TC, T], f32r, arena + 16384)
        YT = at("YT", [P, TC, D], fp32, arena + 28672)
        XH = at("XH", [P, TC, D], f32r, arena + 45056)
        YG = [[at(f"YG{i}{j}", [P, D], fp32, arena + 8192 * i + 4096 * j) for j in range(2)] for i in range(2)]
        assert arena + 45056 + 16384 <= nc.sbuf_usable_end
        PS = ctx.enter_context(nc.psum_tensor("PS", [P, 8, 512], fp32))

        w_in = a["w_in"].rearrange("l (k p) n -> l p k n", p=P)
        w_mod = a["w_mod"].rearrange("l (k p) n -> l p k n", p=P)
        w_uq = a["w_uq"].rearrange("l (k p) n -> l p k n", p=P)
        w_ukv = a["w_ukv"].rearrange("l (k p) n -> l p k n", p=P)
        w_o = a["w_o"].rearrange("l (k p) n -> l p k n", p=P)
        x_d = a["x"].rearrange("b (i p) d -> p (b i) d", p=P)
        out_d = out.rearrange("b (i p) d -> p (b i) d", p=P)
        up_w = [[a["ffn_w_gate"], a["ffn_w_up"]], [a["exp_w_gate"][0], a["exp_w_up"][0]]]
        up_w = [[w.rearrange("e (k p) f -> p (e k) f", p=P) for w in pair] for pair in up_w]
        dn_w = [a["ffn_w_down"], a["exp_w_down"][0]]
        dn_w = [w.rearrange("e (k p) d -> p (e k) d", p=P) for w in dn_w]

        raw_ready = [sem(f"raw_ready{i}") for i in range(RING)]
        rounded, split, unit_used = sem("rounded"), sem("split"), sem("unit_used")

        def load(eng, c, d6, src, k, n):
            if c >= RING:
                eng.wait_ge(split, c - RING + 1 + RING * d6)
            dst = RAW[c % RING][:, 0:k * n].rearrange("p (k n) -> p k n", k=k)
            eng.dma_start(dst, src).then_inc(raw_ready[c % RING], 16)

        def round_unit(eng, c, d6, n=UNIT):
            s = c % RING
            eng.wait_ge(raw_ready[s], 16 * (c // RING + 1 + d6))
            if c >= RING:
                eng.wait_ge(unit_used, c - RING + 1 + RING * d6)
            eng.activation(WH[s][:, 0:n], RAW[s][:, 0:n], ACT.Copy).then_inc(rounded, 1)

        def rest_unit(eng, c, d6, n=UNIT):
            s = c % RING
            eng.wait_ge(rounded, c + 1 + RING * d6)
            eng.tensor_tensor(WL[s][:, 0:n], RAW[s][:, 0:n], WH[s][:, 0:n].bitcast(fp32), SUB).then_inc(split, 1)

        def win_cols(c):
            return min(512, IN_W - 512 * c)

        UP_COLS = [480, 96, 512, 256]

        def unit_cols(l, n):
            if n < 20:
                return 2 * win_cols(n // 4)
            return 2 * UP_COLS[n - 20] if n < 24 else UNIT

        te_t, te_a, te_h, te_l = sem("te_transposed"), sem("te_scaled"), sem("te_rounded"), sem("te_split")
        TE = {}
        for l in range(NL):
            for j, (stage, _) in enumerate([("h1", 8), ("c", 4), ("o", 8), ("h2", 8)]):
                TE[stage, l] = 28 * l + [0, 8, 12, 20][j]
        TE_X = 28 * NL

        def te_scale(eng, m, md, bank, n, scale, bias=0.0):
            eng.wait_ge(te_t, m + 1 + md)
            if m >= 2:
                eng.wait_ge(te_l, m - 1 + md)
            eng.activation(TMP[:, m % 2, 0:n], PS[:, bank, 0:n], ACT.Identity, bias=bias, scale=scale).then_inc(te_a, 1)

        def te_split(eng, m, md, k, n):
            eng.wait_ge(te_a, m + 1 + md)
            eng.tensor_copy(HTH[:, k, 0:n], TMP[:, m % 2, 0:n]).then_inc(te_h, 1)
            eng.wait_ge(te_h, m + 1 + md)
            eng.tensor_tensor(HTL[:, k, 0:n], TMP[:, m % 2, 0:n], HTH[:, k, 0:n].bitcast(fp32), SUB).then_inc(te_l, 1)

        def te_transposes(eng, m, bank, srcs):
            for i, s in enumerate(srcs):
                ins = eng.transpose(PS[:, bank, i * P:(i + 1) * P], s, ident)
            ins.then_inc(te_t, 1)

        modw_ready = [sem("modw_ready0"), sem("modw_ready1")]
        modw_used, macc_init, macc_zero = sem("modw_used"), sem("macc_init"), sem("macc_zero")
        mod_red, mod_out = sem("mod_reduced"), sem("mod_out")
        MOD_WHEN = {(0, 0): [2], (0, 1): [3], (0, 2): [4], (0, 3): [5], (0, 4): [6, 7],
                    (1, 0): [8], (1, 1): [9], (1, 2): [10], (1, 3): [11], (1, 4): []}

        def mod_bank(c, j):
            return ((c + 1) % 2) * 4 + (2 if c < 4 else j * 2)

        def mod_load(eng, q):
            l, s = divmod(q, 6)
            if q >= 2:
                eng.wait_ge(mod_red, q - 1)
            eng.memset(MACC[q % 2][:, :], 0.0).then_inc(macc_zero, 1)
            eng.wait_ge(macc_zero, q + 1)
            eng.dma_start(MACC[q % 2][0:1, :], a["b_mod"][l:l + 1, s * D:(s + 1) * D]).then_inc(macc_init, 16)
            for k in range(DC):
                m = 8 * q + k
                if m >= 2:
                    eng.wait_ge(modw_used, m - 1)
                eng.dma_start(MODW[m % 2][:, :], w_mod[l, :, k, s * D:(s + 1) * D]).then_inc(modw_ready[m % 2], 16)

        def mod_sum(eng, q):
            eng.wait_ge(macc_init, 16 * (q + 1))
            for k in range(DC):
                m = 8 * q + k
                eng.wait_ge(modw_ready[m % 2], 16 * (m // 2 + 1))
                if m:
                    eng.wait_ge(modw_used, m)
                eng.scalar_tensor_tensor(out=MACC[q % 2][:, :], in0=MODW[m % 2][:, :], scalar=CACT[:, k:k + 1],
                                         in1=MACC[q % 2][:, :], op0=MUL, op1=ADD).then_inc(modw_used, 1)

        def mod_reduce(eng, q, bank):
            eng.wait_ge(modw_used, 8 * (q + 1))
            if q % 3 == 2:
                for h in range(2):
                    ins = eng.matmul(PS[:, bank + h, :], ones, MACC[q % 2][:, h * 512:(h + 1) * 512],
                                     start=True, stop=True)
            else:
                for j in range(DC):
                    ins = eng.matmul(PS[:, bank, j:j + 1], MACC[q % 2][:, j * P:(j + 1) * P], ones[:, 0:1],
                                     start=True, stop=True)
            ins.then_inc(mod_red, 1)

        def mod_take(eng, q, bank):
            l, s = divmod(q, 6)
            eng.wait_ge(mod_red, q + 1)
            if s % 3 == 2:
                ins = eng.tensor_scalar(GB[:, s // 3, :], PS[:, bank:bank + 2, :], 1.0, None, ADD)
            else:
                ins = eng.tensor_scalar(MODC[:, 4 * l + 2 * (s // 3) + s % 3, :], PS[:, bank, 0:DC],
                                        float(s % 3), None, ADD)
            ins.then_inc(mod_out, 1)

        def shift_col(l, j, k):
            return MODC[:, 4 * l + 2 * j, k:k + 1]

        def scale_col(l, j, k):
            return MODC[:, 4 * l + 2 * j + 1, k:k + 1]

        loads = sem("first_loads")
        vrow_t, vcol = sem("vrow_transposed"), sem("vcol")
        z_out = sem("z_out")
        gate_n, gate_l, gate_f, gate_s, gate_q = (sem("gate_" + s) for s in ("neg", "log", "f", "sum", "q"))
        ssq, rstd_s, rstd, cn_done, kr_done = (sem(s) for s in ("ct_squares", "ct_sqrt", "ct_rstd", "ct_norm", "k_rope"))
        conv_done, wcv_load, uc, shifted, pool_step = (sem(s) for s in ("conv", "wconv_load", "conv_u", "conv_shifted", "pool_step"))
        up_out, rope_done = sem("up_out"), sem("roped")
        ones_set = sem("ones_set")
        A = {s: sem("att_" + s) for s in ("staged", "tq", "tk", "qev", "kev", "score", "mask", "max", "exp", "tp", "pev", "pv", "rd", "oev")}
        osq, on_sum, on_sqrt, on_rd, on_done = (sem("on_" + s) for s in ("sq", "sum", "sqrt", "rd", "done"))
        ln_v, ln_s, ln_n, ln_x, lnr_load = (sem("ln_" + s) for s in ("var", "sqrt", "norm", "x", "rows"))
        ln_bn, ln_aff = sem("ln_bn"), sem("ln_affine")
        dve = sem("dve_step")
        steps = {"dve": 0}

        def ATT(l, g):
            return HEADS * (2 * l + g)

        def stage_head(eng, hb, h, p, K, wait):
            if wait:
                eng.wait_ge(A["tk"], hb - 1)
            eng.tensor_copy(SQ[p][:, :, 0:K], QA[:, ds(h, 1), :, 0:K])
            eng.tensor_copy(SK[p][:, :, 0:K], KA[:, ds(h, 1), :, 0:K]).then_inc(A["staged"], 1)

        def att_tq(eng, hb, p, K, first=False):
            eng.wait_ge(A["staged"], hb + 1)
            if not first:
                eng.wait_ge(A["kev"], hb)
            for i in range(TC):
                ins = eng.transpose(PS[0:K, 6, i * P:(i + 1) * P], SQ[p][:, i, 0:K], ident)
            ins.then_inc(A["tq"], 1)

        def att_tk(eng, hb, p, K):
            eng.wait_ge(A["qev"], hb + 1)
            for i in range(TC):
                ins = eng.transpose(PS[0:K, 6, i * P:(i + 1) * P], SK[p][:, i, 0:K], ident)
            ins.then_inc(A["tk"], 1)

        def att_score(eng, hb, i, p, K, first=False):
            if i == 0:
                eng.wait_ge(A["kev"], hb + 1)
            if not first:
                eng.wait_ge(A["exp"], 4 * hb - 3 + i)
            eng.matmul(PS[:, i, 0:(i + 1) * P], QT[p][0:K, i * P:(i + 1) * P], KT[p][0:K, 0:(i + 1) * P],
                       start=True, stop=True).then_inc(A["score"], 1)

        def att_tp(eng, hb, i, wait=True):
            eng.wait_ge(A["exp"], 4 * hb + i + 1)
            if wait:
                eng.wait_ge(A["pev"], 4 * hb + i - 1)
            for j in range(i + 1):
                ins = eng.transpose(PS[:, 4 + i % 2, j * P:(j + 1) * P], PR[i % 2][:, j * P:(j + 1) * P], ident)
            ins.then_inc(A["tp"], 1)

        def att_pv(eng, hb, h, i, p, wait):
            eng.wait_ge(A["pev"], 4 * hb + i + 1)
            if i == 0 and wait:
                eng.wait_ge(A["oev"], hb)
            c = p * 256 + i * HD
            for j in range(i + 1):
                ins = eng.matmul(PS[:, 7, c:c + HD], PTS[i % 2][:, j * P:(j + 1) * P], VA[:, ds(h, 1), j, :],
                                 start=(j == 0), stop=(j == i))
            ins.then_inc(A["pv"], 1)

        def att_pe(eng, l, g):
            K, b = (HD + 2, KQ_MLA)[g], ATT(l, g)

            def head(hb, h, p, last=False, first=False):
                w = not (first and b == 0)
                att_tp(eng, hb, 0, w)
                if not last:
                    att_tq(eng, hb + 1, 1 - p, K)
                att_tp(eng, hb, 1, w)
                att_pv(eng, hb, h, 0, p, w)
                if not last:
                    att_tk(eng, hb + 1, 1 - p, K)
                att_tp(eng, hb, 2)
                att_pv(eng, hb, h, 1, p, w)
                if not last:
                    att_score(eng, hb + 1, 0, 1 - p, K)
                    att_score(eng, hb + 1, 1, 1 - p, K)
                att_tp(eng, hb, 3)
                att_pv(eng, hb, h, 2, p, w)
                if not last:
                    att_score(eng, hb + 1, 2, 1 - p, K)
                    att_score(eng, hb + 1, 3, 1 - p, K)
                att_pv(eng, hb, h, 3, p, w)

            if g == 0:
                eng.wait_ge(gate_q, 2 * (l + 1))
                eng.wait_ge(te_l, TE["c", l] + 4)
            else:
                eng.wait_ge(up_out, 16 * (l + 1))
            att_tq(eng, b, 0, K, first=True)
            att_tk(eng, b, 0, K)
            for i in range(TC):
                att_score(eng, b, i, 0, K, first=(b == 0))
            head(b, 0, 0, first=True)
            with eng.Fori(0, 2) as it:
                head(b + 1 + 2 * it, 1 + 2 * it, 1)
                head(b + 2 + 2 * it, 2 + 2 * it, 0)
            head(b + 5, 5, 1, last=True)

        def att_act(eng, l, g):
            K, b = (HD + 2, KQ_MLA)[g], ATT(l, g)

            def qev(hb, p):
                eng.wait_ge(A["tq"], hb + 1)
                eng.copy(QT[p][0:K, :], PS[0:K, 6, :]).then_inc(A["qev"], 1)

            def exp(hb, i, p, wait=True):
                eng.wait_ge(A["max"], 4 * hb + i + 1)
                if wait:
                    eng.wait_ge(A["tp"], 4 * hb + i - 1)
                n = (i + 1) * P
                eng.activation(PR[i % 2][:, 0:n], PS[:, i, 0:n], ACT.Exp, bias=NM[:, p, i:i + 1],
                               accum_out=RSUM[:, p, i:i + 1]).then_inc(A["exp"], 1)

            def pev(hb, i, wait=True):
                eng.wait_ge(A["tp"], 4 * hb + i + 1)
                if wait:
                    eng.wait_ge(A["pv"], 4 * hb + i - 1)
                n = (i + 1) * P
                eng.copy(PTS[i % 2][:, 0:n], PS[:, 4 + i % 2, 0:n]).then_inc(A["pev"], 1)

            def head(hb, p, last=False, first=False):
                w = not (first and b == 0)
                exp(hb, 0, p, w)
                exp(hb, 1, p, w)
                pev(hb, 0, w)
                if not last:
                    qev(hb + 1, 1 - p)
                exp(hb, 2, p)
                pev(hb, 1, w)
                exp(hb, 3, p)
                pev(hb, 2)
                pev(hb, 3)

            if g == 0:
                eng.wait_ge(conv_done, l + 1)
            qev(b, 0)
            head(b, 0, first=True)
            with eng.Fori(0, 2) as it:
                head(b + 1 + 2 * it, 1)
                head(b + 2 + 2 * it, 0)
            head(b + 5, 1, last=True)

        def att_dve(eng, l, g):
            K, b = (HD + 2, KQ_MLA)[g], ATT(l, g)

            def kev(hb, p):
                eng.wait_ge(A["tk"], hb + 1)
                eng.tensor_copy(KT[p][0:K, :], PS[0:K, 6, :]).then_inc(A["kev"], 1)

            def soft(hb, i, p):
                eng.wait_ge(A["score"], 4 * hb + i + 1)
                diag = PS[:, i, i * P:(i + 1) * P]
                eng.tensor_tensor(diag, diag, CST[:, C_MASK:C_MASK + P], ADD).then_inc(A["mask"], 1)
                eng.wait_ge(A["mask"], 4 * hb + i + 1)
                eng.tensor_reduce(NM[:, p, i:i + 1], PS[:, i, 0:(i + 1) * P], AX.X, MAX, negate=True).then_inc(A["max"], 1)

            def take(hb, h, p):
                eng.wait_ge(A["pv"], 4 * hb + 4)
                eng.reciprocal(RD[:, p, :], RSUM[:, p, :]).then_inc(A["rd"], 1)
                eng.wait_ge(A["rd"], hb + 1)
                o = PS[:, 7, p * 256:(p + 1) * 256].rearrange("p (i d) -> p i d", d=HD)
                eng.tensor_tensor(OA[:, :, ds(h + HEADS * g, 1), :], o, RD[:, p, :].unsqueeze(2).to_broadcast([P, TC, HD]),
                                  MUL).then_inc(A["oev"], 1)

            def head(hb, h, p, last=False, first=False):
                soft(hb, 0, p)
                soft(hb, 1, p)
                if not first:
                    take(hb - 1, h - 1, 1 - p)
                soft(hb, 2, p)
                soft(hb, 3, p)
                if not last:
                    kev(hb + 1, 1 - p)

            kev(b, 0)
            head(b, 0, 0, first=True)
            with eng.Fori(0, 2) as it:
                head(b + 1 + 2 * it, 1 + 2 * it, 1)
                head(b + 2 + 2 * it, 2 + 2 * it, 0)
            head(b + 5, 5, 1, last=True)
            take(b + 5, 5, 1)

        def att_pool(eng, l, g):
            K, b = (HD + 2, KQ_MLA)[g], ATT(l, g)
            if g == 0:
                eng.wait_ge(z_out, 20 * (l + 1))
                eng.wait_ge(gate_q, 2 * (l + 1))
                eng.wait_ge(kr_done, 2 * (l + 1))
            else:
                eng.wait_ge(up_out, 16 * (l + 1))
                eng.wait_ge(rope_done, 3 * (l + 1))
            stage_head(eng, b, 0, 0, K, b > 0)
            stage_head(eng, b + 1, 1, 1, K, b > 0)
            with eng.Fori(0, 2) as it:
                stage_head(eng, b + 2 + 2 * it, 2 + 2 * it, 0, K, True)
                stage_head(eng, b + 3 + 2 * it, 3 + 2 * it, 1, K, True)

        def ln_dve(eng, n, src, ready, dst_last=None):
            def tail(i):
                m = 4 * n + i
                eng.wait_ge(ln_n, m + 1)
                if i == 0:
                    eng.wait_ge(lnr_load, 32 * (n + 1))
                eng.tensor_tensor(X[:, i, :], X[:, i, :], LNR[:, 0, :], MUL).then_inc(ln_aff, 1)
                eng.wait_ge(ln_aff, m + 1)
                eng.tensor_tensor(X[:, i, :], X[:, i, :], LNR[:, 1, :], ADD).then_inc(ln_x, 1)

            for i in range(TC):
                m = 4 * n + i
                ready(i)
                if i >= 2:
                    eng.wait_ge(ln_bn, 5 * (m - 2) + 2)
                t = LT[i % 2]
                eng.tensor_tensor(t[:, :].rearrange("p (a b) -> p a b", a=2), src(i),
                                  GB[:, n % 2, :].rearrange("p (a b) -> p a b", a=2), MUL).then_inc(ln_bn, 1)
                eng.wait_ge(ln_bn, 5 * m + 1)
                eng.scalar_tensor_tensor(out=X[:, i, :], in0=X[:, i, :], scalar=ALPHA, in1=t[:, :],
                                         op0=MUL, op1=ADD).then_inc(ln_bn, 1)
                eng.wait_ge(ln_bn, 5 * m + 2)
                for h in range(2):
                    eng.bn_stats(BNS[:, i % 2, 6 * h:6 * h + 6], X[:, i, h * 512:(h + 1) * 512]).then_inc(ln_bn, 1)
                eng.wait_ge(ln_bn, 5 * m + 4)
                if i >= 2:
                    eng.wait_ge(ln_n, m - 1)
                eng.bn_aggr(MV[:, i % 2, :], BNS[:, i % 2, :]).then_inc(ln_bn, 1)
                eng.wait_ge(ln_s, m + 1)
                eng.reciprocal(LNS[:, i % 2, 0:1], LNS[:, i % 2, 0:1]).then_inc(dve, 1)
                steps["dve"] += 1
                eng.wait_ge(dve, steps["dve"])
                eng.scalar_tensor_tensor(out=LNS[:, i % 2, 1:2], in0=MV[:, i % 2, 0:1], scalar=-1.0,
                                         in1=LNS[:, i % 2, 0:1], op0=MUL, op1=MUL).then_inc(ln_v, 1)
                if i:
                    tail(i - 1)
            tail(TC - 1)

        def ln_act(eng, n):
            for i in range(TC):
                m = 4 * n + i
                eng.wait_ge(ln_bn, 5 * m + 5)
                eng.activation(LNS[:, i % 2, 0:1], MV[:, i % 2, 1:2], ACT.Sqrt, bias=CST[:, C_EPS:C_EPS + 1]).then_inc(ln_s, 1)
                eng.wait_ge(ln_v, m + 1)
                eng.activation(X[:, i, :], X[:, i, :], ACT.Identity, bias=LNS[:, i % 2, 1:2],
                               scale=LNS[:, i % 2, 0:1]).then_inc(ln_n, 1)

        def ln_rows(eng, n):
            l, w = divmod(n, 2)
            if w == 0:
                eng.wait_ge(A["oev"], ATT(l, 1) + HEADS)
            elif l == 0:
                eng.wait_ge(acc_done, 1)
            else:
                eng.wait_ge(y_st, CLEARED + 16 * NE)
            for j, name in enumerate((f"ln{w + 1}_g", f"ln{w + 1}_b")):
                eng.dma_start(LNR[:, j, :], a[name][l:l + 1, :].to_broadcast([P, D])).then_inc(lnr_load, 16)

        silu_done, hm_done, hh_done, hl_done = (sem(s) for s in ("silu", "h_product", "h_rounded", "h_split"))
        dpart, dtaken, acc_done = sem("down_part"), sem("down_taken"), sem("acc_done")
        y_t, y_out, y_st = sem("y_transposed"), sem("y_out"), sem("y_stored")
        CLEARED = 16 * 4
        sel_done, zero_done = sem("sel_done"), sem("zero_done")

        class Swi:
            def __init__(s, base, G, gb, x, e=0):
                s.base, s.G, s.gb, s.x, s.e = base, G, gb + G * e, x + e, e

            def unit(s, g, j):
                return s.base + 4 + j, s.G * s.e + g - 1

            def unit0(s, j):
                return s.base + j, s.G * s.e

            def last(s, j):
                return s.base + 4 + j, s.G * s.e + s.G - 1

        def used_at(c_d):
            c, d = c_d
            return c + 1 + RING * d

        def swi_pe(eng, sw, N):
            small = N <= 256
            xh, xl = HTH, HTL

            def gate_up(g, units, first):
                for w in range(2):
                    for half in range(2):
                        c, d = units(2 * w + half)
                        if half == 0 and not first:
                            eng.wait_ge(hm_done if w else silu_done, sw.gb + g)
                        eng.wait_ge(split, used_at((c, d)))
                        s = c % RING
                        for fc in range(2):
                            for kk in range(4):
                                k, o = 4 * half + kk, kk * 256 + fc * P
                                for j, (wt, xt) in enumerate(((WH, xh), (WL, xh), (WH, xl))):
                                    ins = eng.matmul(PS[:, 2 * w + fc, 0:N], wt[s][:, o:o + P], xt[:, k, 0:N],
                                                     start=(k == 0 and j == 0), stop=(k == DC - 1 and j == 2))
                        ins.then_inc(unit_used, 1)

            def down(g, units):
                (c0, d0), (c1, d1) = units(4), units(5)
                eng.wait_ge(hl_done, sw.gb + g + 1)
                eng.wait_ge(split, used_at((c1, d1)))
                for dc in range(DC):
                    if small:
                        o = PS[:, 4 + dc // 2, dc % 2 * 256:dc % 2 * 256 + N]
                    else:
                        eng.wait_ge(dtaken, DC * (sw.gb + g) + DC + dc - 3)
                        o = PS[:, 4 + dc % 4, 0:N]
                    for fc, c in enumerate((c0, c1)):
                        s = c % RING
                        for j, (wt, ht) in enumerate(((WH, HAH), (WL, HAH), (WH, HAL))):
                            ins = eng.matmul(o, wt[s][:, dc * P:(dc + 1) * P], ht[:, fc, 0:N],
                                             start=(not small and fc == 0 and j == 0),
                                             stop=(not small and fc == 1 and j == 2), skip_group_check=small)
                        if dc == DC - 1 and fc == 0:
                            ins.then_inc(unit_used, 1)
                    if not small and dc < DC - 1:
                        ins.then_inc(dpart, 1)
                if small:
                    ins.then_inc(unit_used, 1)
                else:
                    ins.then_inc(dpart, 1)
                    eng.wait_ge(dpart, DC * (sw.gb + g + 1))
                    eng.sem_inc(unit_used, 1)

            if small:
                for b in range(4):
                    ins = eng.matmul(PS[:, 4 + b, :], ZERO[:, 0:P], ZERO[:, :], start=True, stop=False,
                                     skip_group_check=True)
                ins.then_inc(dpart, DC * sw.G)
            gate_up(0, sw.unit0, True)
            with eng.Fori(1, sw.G) as g:
                gate_up(g, lambda j: sw.unit(g, j), False)
                down(g - 1, lambda j: sw.unit(g, j))
            down(sw.G - 1, lambda j: sw.last(j - 4))

        def swi_act(eng, sw, N):
            def rounded_h(g):
                eng.wait_ge(hm_done, sw.gb + g + 1)
                eng.activation(HAH[:, :, 0:N], SIL[:, :, 0:N], ACT.Copy).then_inc(hh_done, 1)

            def body(g, first):
                for j in range(2):
                    round_unit(eng, *sw.unit(g, j))
                silu0(g - 1, first)
                for j in range(2, 4):
                    round_unit(eng, *sw.unit(g, j))
                if not first:
                    eng.wait_ge(unit_used, used_at(sw.unit(g - 1, 5)))
                rounded_h(g - 1)
                for j in range(4, 6):
                    round_unit(eng, *sw.unit(g, j))

            def silu0(g, first):
                if first:
                    eng.wait_ge(unit_used, used_at(sw.unit0(1)))
                else:
                    eng.wait_ge(hl_done, sw.gb + g)
                    eng.wait_ge(unit_used, used_at(sw.unit(g, 1)))
                eng.activation(SIL[:, :, 0:N], PS[:, 0:2, 0:N], ACT.Silu).then_inc(silu_done, 1)

            for j in range(4):
                round_unit(eng, *sw.unit0(j))
            body(1, True)
            with eng.Fori(2, sw.G) as g:
                body(g, False)
            silu0(sw.G - 1, False)
            eng.wait_ge(unit_used, used_at(sw.unit(sw.G - 1, 5)))
            rounded_h(sw.G - 1)
            for j in range(2):
                round_unit(eng, *sw.last(j))

        def swi_dve(eng, sw, N):
            small = N <= 256

            def product(g):
                eng.wait_ge(silu_done, sw.gb + g + 1)
                up = PS[:, 2:4, 0:N]
                eng.tensor_tensor(SIL[:, :, 0:N], SIL[:, :, 0:N], up, MUL).then_inc(hm_done, 1)

            def low_h(g):
                eng.wait_ge(hh_done, sw.gb + g + 1)
                eng.tensor_tensor(HAL[:, :, 0:N], SIL[:, :, 0:N], HAH[:, :, 0:N].bitcast(fp32), SUB).then_inc(hl_done, 1)

            def take_down(g, units):
                for dc in range(DC):
                    eng.wait_ge(dpart, DC * (sw.gb + g) + dc + 1)
                    eng.tensor_tensor(ACC[:, dc, 0:N], ACC[:, dc, 0:N], PS[:, 4 + dc % 4, 0:N], ADD).then_inc(dtaken, 1)

            def body(g, first):
                for j in range(4):
                    rest_unit(eng, *sw.unit(g, j))
                if not first and not small:
                    take_down(g - 2, None)
                eng.wait_ge(unit_used, used_at(sw.unit0(3) if first else sw.unit(g - 1, 3)))
                product(g - 1)
                for j in range(4, 6):
                    rest_unit(eng, *sw.unit(g, j))
                low_h(g - 1)

            if not small:
                eng.memset(ACC[:, :, 0:N], 0.0).then_inc(dve_acc, 1)
                eng.wait_ge(dve_acc, sw.x + 1)
            for j in range(4):
                rest_unit(eng, *sw.unit0(j))
            body(1, True)
            with eng.Fori(2, sw.G) as g:
                body(g, False)
            if not small:
                take_down(sw.G - 2, None)
            eng.wait_ge(unit_used, used_at(sw.unit(sw.G - 1, 3)))
            product(sw.G - 1)
            for j in range(2):
                rest_unit(eng, *sw.last(j))
            low_h(sw.G - 1)
            if small:
                eng.wait_ge(unit_used, used_at(sw.last(1)))
                for b in range(4):
                    ins = eng.tensor_copy(ACC[:, 2 * b:2 * b + 2, 0:N],
                                          PS[:, 4 + b, :].rearrange("p (a n) -> p a n", a=2)[:, :, 0:N])
                ins.then_inc(dtaken, DC * sw.G)
            else:
                take_down(sw.G - 1, None)
            if small:
                eng.sem_inc(dve_acc, 1)
            eng.wait_ge(dtaken, DC * (sw.gb + sw.G + 1))
            eng.sem_inc(acc_done, 1)

        dve_acc, ht_done = sem("acc_cleared"), sem("h_transposed")

        def narrow_pe(eng, sw):
            def gate_up(g, units, w, first):
                for half in range(2):
                    c, d = units(2 * w + half)
                    if half == 0 and not first:
                        eng.wait_ge(hm_done if w else silu_done, sw.gb + g)
                    eng.wait_ge(split, used_at((c, d)))
                    s = c % RING
                    for kk in range(4):
                        k = 4 * half + kk
                        for j, (xt, wt) in enumerate(((HTH, WH), (HTH, WL), (HTL, WH))):
                            ins = eng.matmul(PS[:, 2 * w, 0:256], xt[:, k, 0:P], wt[s][:, kk * 256:(kk + 1) * 256],
                                             start=(k == 0 and j == 0), stop=(k == DC - 1 and j == 2))
                    ins.then_inc(unit_used, 1)

            def turn(g):
                eng.wait_ge(hm_done, sw.gb + g + 1)
                for fc in range(2):
                    ins = eng.transpose(PS[:, 1, fc * P:(fc + 1) * P], SIL[:, 0, fc * P:(fc + 1) * P], ident)
                ins.then_inc(ht_done, 1)

            def down(g, units):
                eng.wait_ge(hl_done, sw.gb + g + 1)
                for fc in range(2):
                    c, d = units(4 + fc)
                    eng.wait_ge(split, used_at((c, d)))
                    for ht, wt in ((HAH, WH), (HAH, WL), (HAL, WH)):
                        for h in range(2):
                            ins = eng.matmul(PS[:, 4 + h, :], ht[:, fc, 0:P], wt[c % RING][:, h * 512:(h + 1) * 512],
                                             start=False, stop=False, skip_group_check=True)
                    ins.then_inc(unit_used, 1)

            for b in range(2):
                ins = eng.matmul(PS[:, 4 + b, :], ZERO[:, 0:P], ZERO[:, :], start=True, stop=False,
                                 skip_group_check=True)
            ins.then_inc(dpart, DC * sw.G)
            for w in range(2):
                gate_up(0, sw.unit0, w, True)
            with eng.Fori(1, sw.G) as g:
                gate_up(g, lambda j: sw.unit(g, j), 0, False)
                turn(g - 1)
                gate_up(g, lambda j: sw.unit(g, j), 1, False)
                down(g - 1, lambda j: sw.unit(g, j))
            turn(sw.G - 1)
            down(sw.G - 1, lambda j: sw.last(j - 4))
            eng.sem_inc(y_t, 4)

        def narrow_act(eng, sw):
            def silu(g, gate):
                eng.wait_ge(unit_used, gate)
                eng.activation(SIL[:, 0, 0:256], PS[:, 0, 0:256], ACT.Silu).then_inc(silu_done, 1)

            def rounded_h(g):
                eng.wait_ge(ht_done, sw.e * sw.G + g + 1)
                eng.activation(HAH[:, :, 0:P], PS[:, 1, 0:256].rearrange("p (f n) -> p f n", n=P), ACT.Copy).then_inc(hh_done, 1)

            def body(g, first):
                for j in range(2):
                    round_unit(eng, *sw.unit(g, j))
                if not first:
                    eng.wait_ge(hl_done, sw.gb + g - 1)
                silu(g - 1, used_at(sw.unit0(1) if first else sw.unit(g - 1, 1)))
                for j in range(2, 4):
                    round_unit(eng, *sw.unit(g, j))
                if not first:
                    eng.wait_ge(unit_used, used_at(sw.unit(g - 1, 5)))
                rounded_h(g - 1)
                for j in range(4, 6):
                    round_unit(eng, *sw.unit(g, j))

            for j in range(4):
                round_unit(eng, *sw.unit0(j))
            body(1, True)
            with eng.Fori(2, sw.G) as g:
                body(g, False)
            eng.wait_ge(hl_done, sw.gb + sw.G - 1)
            silu(sw.G - 1, used_at(sw.unit(sw.G - 1, 1)))
            eng.wait_ge(unit_used, used_at(sw.unit(sw.G - 1, 5)))
            rounded_h(sw.G - 1)
            for j in range(2):
                round_unit(eng, *sw.last(j))

        def narrow_dve(eng, sw):
            def product(g, up):
                eng.wait_ge(silu_done, sw.gb + g + 1)
                eng.wait_ge(unit_used, up)
                eng.tensor_tensor(SIL[:, 0, 0:256], SIL[:, 0, 0:256], PS[:, 2, 0:256], MUL).then_inc(hm_done, 1)

            def low_h(g):
                eng.wait_ge(hh_done, sw.gb + g + 1)
                eng.tensor_tensor(HAL[:, :, 0:P], PS[:, 1, 0:256].rearrange("p (f n) -> p f n", n=P),
                                  HAH[:, :, 0:P].bitcast(fp32), SUB).then_inc(hl_done, 1)

            def body(g, first):
                for j in range(2):
                    rest_unit(eng, *sw.unit(g, j))
                product(g - 1, used_at(sw.unit0(3) if first else sw.unit(g - 1, 3)))
                for j in range(2, 4):
                    rest_unit(eng, *sw.unit(g, j))
                low_h(g - 1)
                for j in range(4, 6):
                    rest_unit(eng, *sw.unit(g, j))

            for j in range(4):
                rest_unit(eng, *sw.unit0(j))
            body(1, True)
            with eng.Fori(2, sw.G) as g:
                body(g, False)
            product(sw.G - 1, used_at(sw.unit(sw.G - 1, 3)))
            low_h(sw.G - 1)
            for j in range(2):
                rest_unit(eng, *sw.last(j))
            eng.sem_inc(dve_acc, 1)
            eng.sem_inc(dtaken, DC * sw.G)
            eng.sem_inc(acc_done, 1)


        def swi_load(eng, kind, sw):
            up, dn = up_w[kind], dn_w[kind]
            e = sw.e

            def gu(units, g):
                for w in range(2):
                    for half in range(2):
                        load(eng, *units(2 * w + half), up[w][:, ds(e * DC + 4 * half, 4), ds(g * 256, 256)], 4, 256)

            def dn_(units, g):
                for fc in range(2):
                    load(eng, *units(4 + fc), dn[:, ds(e * 2 * sw.G + 2 * g + fc, 1), :], 1, D)

            gu(sw.unit0, 0)
            with eng.Fori(1, sw.G) as g:
                gu(lambda j: sw.unit(g, j), g)
                dn_(lambda j: sw.unit(g, j), g - 1)
            dn_(lambda j: sw.last(j - 4), sw.G - 1)

        def by_width(eng, count, body, widths=WIDTHS):
            if len(widths) == 1:
                body(widths[0])
                return
            with eng.If(count <= widths[0]):
                body(widths[0])
            with eng.Else():
                by_width(eng, count, body, widths[1:])

        routed = sem("routed")

        def expert(eng, engine_body):
            with eng.Fori(0, NE) as e:
                count = eng.value_load(CNT[0:1, ds(e, 1)], min_val=0, max_val=T)
                sw = Swi(SWI_BASE[1], EXP_G, FFN_G, 1, e)
                by_width(eng, count, lambda N: engine_body(sw, e, N))

        block = ctx.enter_context(nc.Block())

        @block.sync
        def _(sp):
            sp.dma_start(CST[:, :], a["consts"]).then_inc(loads, 16)
            sp.dma_start(VROW[0:8, :], a["c"].rearrange("b (k p) -> (b k) p", p=P)).then_inc(loads, 16)
            sp.dma_start(VROW[8:12, :], a["q_norm_g"].rearrange("l (k p) -> (l k) p", p=P)).then_inc(loads, 16)
            sp.dma_start(VROW[12:16, :], a["kv_norm_g"].rearrange("l (k p) -> (l k) p", p=P)).then_inc(loads, 16)
            sp.dma_start(VROW[16:32, :], a["head_norm_g"].rearrange("l (k p) -> (l k) p", p=P)).then_inc(loads, 16)
            sp.dma_start(X[:, :, :], x_d).then_inc(loads, 16)
            for l in range(NL):
                sp.dma_start(BF[:, l, :], a["b_fgate"][l:l + 1, :].to_broadcast([P, HEADS])).then_inc(loads, 16)
            sp.dma_start(RW[:, :, :], a["router_w"][0].rearrange("(k p) e -> p k e", p=P)).then_inc(loads, 16)
            sp.wait_ge(modw_used, 12)
            for l in range(NL):
                b = BASE[l]
                for c in range(5):
                    n = win_cols(c)
                    for u in range(4):
                        load(sp, b + 4 * c + u, 0, w_in[l, :, 2 * u:2 * u + 2, 512 * c:512 * c + n], 2, n)
                for j, (w, o) in enumerate(((w_uq, 0), (w_uq, 480), (w_ukv, 0), (w_ukv, 512))):
                    load(sp, b + 20 + j, 0, w[l, :, :, o:o + UP_COLS[j]], 2, UP_COLS[j])
                for half in range(2):
                    for u in range(4):
                        load(sp, b + 24 + 4 * half + u, 0, w_o[l, :, O_CHUNKS[u], half * 512:(half + 1) * 512], 2, 512)
                if l == 0:
                    swi_load(sp, 0, Swi(SWI_BASE[0], FFN_G, 0, 0))
                else:
                    with sp.Fori(0, NE) as e:
                        swi_load(sp, 1, Swi(SWI_BASE[1], EXP_G, FFN_G, 1, e))
            for i in range(TC):
                sp.wait_ge(ln_x, 12 + i + 1)
                sp.dma_start(out_d[:, i, :], X[:, i, :]).then_inc(sem("out_stored"), 16)
            sp.wait_ge(sem("out_stored"), 16 * TC)

        @block.gpsimd
        def _(pool):
            step = [0]

            def link(ins):
                step[0] += 1
                ins.then_inc(pool_step, 1)
                pool.wait_ge(pool_step, step[0])

            mod_load(pool, 0)
            mod_load(pool, 1)
            for l in range(NL):
                if l:
                    pool.wait_ge(ln_x, 8)
                pool.memset(QA[:, :, :, HD + 1:HD + 2], 1.0)
                pool.memset(KA[:, :, :, HD:HD + 1], 1.0).then_inc(ones_set, 1)
                for c in range(5):
                    for q in MOD_WHEN[l, c]:
                        if l == 1:
                            pool.wait_ge(te_t, TE["o", 0] + 8)
                        mod_load(pool, q)
                pool.wait_ge(z_out, 20 * (l + 1))
                pool.wait_ge(modw_used, 8 * (8 if l == 0 else 12))
                pool.dma_start(WCV[:, :, :], a["w_conv"][l:l + 1, :, :].rearrange("l k c -> l (k c)").to_broadcast([P, 768])
                               .rearrange("p (k c) -> p k c", k=3)).then_inc(wcv_load, 16)
                ZCc, Zh, Zb = ZR[:, :, ZC:ZC + 256], ZR[:, :, ZH:ZH + 256], ZR[:, :, ZB:ZB + 256]
                pool.memset(U1[0:1, 0, :], 0.0)
                pool.memset(U2[0:2, 0, :], 0.0)
                link(pool.tensor_tensor(ZCc, ZCc, Zh, MUL))
                for s, U in ((1, U1), (2, U2)):
                    pool.dma_start(U[s:112 + s, :, :], ZR[0:112, :, ZC:ZC + 256]).then_inc(shifted, 16)
                    pool.dma_start(U[112 + s:P, :, :], ZR[112:P - s, :, ZC:ZC + 256]).then_inc(shifted, 16)
                    pool.dma_start(U[0:s, 1:TC, :], ZR[P - s:P, 0:TC - 1, ZC:ZC + 256]).then_inc(shifted, 16)
                oc = OA[:, :, 12:16, :].rearrange("p i h d -> p i (h d)")

                def tap(k):
                    return WCV[:, k:k + 1, :].to_broadcast([P, TC, 256])
                pool.wait_ge(wcv_load, 16 * (l + 1))
                pool.wait_ge(mod_red, 8 if l == 0 else 12)
                link(pool.tensor_tensor(Zh, ZCc, tap(2), MUL))
                pool.wait_ge(shifted, 96 * (l + 1))
                pool.tensor_tensor(U1[:, :, :], U1[:, :, :], tap(1), MUL)
                link(pool.tensor_tensor(U2[:, :, :], U2[:, :, :], tap(0), MUL))
                link(pool.tensor_tensor(Zh, Zh, U1[:, :, :], ADD))
                link(pool.tensor_tensor(Zh, Zh, U2[:, :, :], ADD))
                pool.tensor_tensor(oc, Zh, Zb, MUL).then_inc(conv_done, 1)
                pool.wait_ge(conv_done, l + 1)
                att_pool(pool, l, 0)
                att_pool(pool, l, 1)
                ln_rows(pool, 2 * l)
                if l == 0:
                    ln_rows(pool, 1)
            ln_rows(pool, 3)
            pool.wait_ge(routed, 2)
            for i in range(TC):
                if i >= 2:
                    pool.wait_ge(ln_bn, 5 * (12 + i - 2) + 1)
                else:
                    pool.wait_ge(y_t, 4 * NE)
                for j in range(2):
                    pool.indirect_dma_start(
                        out=YG[i % 2][j][:, :], out_offset=None, in_=ybuf[:, :],
                        in_offset=bass.IndirectOffsetOnAxis(ap=ROWI[:, j, i:i + 1], axis=0)).then_inc(sem(f"y_back{i % 2}"), 16)

        @block.scalar
        def _(act):
            act.wait_ge(vrow_t, 1)
            act.activation(CACT[:, :], PS[:, 0, 0:DC], ACT.Silu).then_inc(y_out, 4)
            act.copy(VCOL[:, :], PS[:, 0, DC:32]).then_inc(vcol, 1)
            for l in range(NL):
                b = BASE[l]
                if l:
                    for n in range(4):
                        round_unit(act, b + n, 0)
                    ln_act(act, 1)
                act.wait_ge(mod_out, 2 if l == 0 else 8)
                for k in range(DC):
                    te_scale(act, TE["h1", l] + k, 0, k, T, scale_col(l, 0, k), shift_col(l, 0, k))

                def z_take(c):
                    for i in range(TC):
                        bank = c % 2 * 4 + i
                        act.wait_ge(unit_used, b + 4 * c + 4)
                        src = PS[:, bank, :]

                        def heads(s, lo, hi):
                            return s[:, lo:hi].rearrange("p (h d) -> p h d", d=HD)
                        if c == 0:
                            act.activation(QA[:, :, i, 0:HD], heads(src, 0, 384), ACT.Copy, scale=HD ** -0.5)
                            ins = act.copy(KA[:, 0:2, i, 0:HD], heads(src, 384, 512))
                        elif c == 1:
                            act.copy(KA[:, 2:6, i, 0:HD], heads(src, 0, 256))
                            ins = act.copy(VA[:, 0:4, i, :], heads(src, 256, 512))
                        elif c == 2:
                            act.copy(VA[:, 4:6, i, :], heads(src, 0, 128))
                            ins = act.copy(ZR[:, i, 0:384], src[:, 128:512])
                        else:
                            n = win_cols(c)
                            ins = act.copy(ZR[:, i, 384 + 512 * (c - 3):384 + 512 * (c - 3) + n], src[:, 0:n])
                        ins.then_inc(z_out, 1)
                for c in range(5):
                    for u in range(4):
                        if l == 0 or c:
                            round_unit(act, b + 4 * c + u, 0, 2 * win_cols(c))
                    if c:
                        z_take(c - 1)
                z_take(4)
                act.wait_ge(gate_n, l + 1)
                act.activation(FG[:, 2, :], FG[:, 1, :], ACT.Exp).then_inc(gate_l, 1)
                act.wait_ge(gate_l, 2 * l + 1)
                act.activation(FG[:, 2, :], FG[:, 2, :], ACT.Ln, bias=1.0).then_inc(gate_l, 1)
                for i in range(TC):
                    for w in range(2):
                        ins = act.activation(CN[:, i, w * 256:(w + 1) * 256], ZR[:, i, ZQ + w * 256:ZQ + (w + 1) * 256],
                                             ACT.Square, accum_out=SS[:, 0, 2 * i + w:2 * i + w + 1])
                ins.then_inc(ssq, 1)
                act.wait_ge(ssq, l + 1)
                act.activation(SS[:, 0, 0:8], SS[:, 0, 0:8], ACT.Sqrt, bias=CST[:, C_EPS + 1:C_EPS + 2],
                               scale=1.0 / 256).then_inc(rstd_s, 1)
                for k in range(4):
                    g = VCOL[:, (0, 4)[k // 2] + 2 * l + k % 2:(0, 4)[k // 2] + 2 * l + k % 2 + 1]
                    te_scale(act, TE["c", l] + k, 0, 4 + k, T, g)
                for j in range(4):
                    round_unit(act, b + 20 + j, 0, 2 * UP_COLS[j])
                att_act(act, l, 0)
                for j in range(4):
                    for i in range(TC):
                        act.wait_ge(unit_used, b + 20 + j + 1)
                        src = PS[:, j % 2 * 4 + i, :]
                        if j == 0:
                            act.wait_ge(A["staged"], ATT(l, 1))
                            ins = act.activation(QA[:, 0:5, i, :], src[:, 0:480].rearrange("p (h d) -> p h d", d=96),
                                                 ACT.Copy, scale=KQ_MLA ** -0.5)
                        elif j == 1:
                            ins = act.activation(QA[:, 5, i, :], src[:, 0:96], ACT.Copy, scale=KQ_MLA ** -0.5)
                        else:
                            h0, h1 = (0, 4) if j == 2 else (4, 6)
                            s = src[:, 0:P * (h1 - h0)].rearrange("p (h d) -> p h d", d=P)
                            act.copy(KA[:, h0:h1, i, 0:HD], s[:, :, 0:HD])
                            ins = act.copy(VA[:, h0:h1, i, :], s[:, :, HD:P])
                        ins.then_inc(up_out, 1)
                for n in range(24, 30):
                    round_unit(act, b + n, 0)
                att_act(act, l, 1)
                act.wait_ge(A["oev"], ATT(l, 1) + HEADS)
                act.wait_ge(conv_done, l + 1)
                for i in range(TC):
                    act.activation(OSQ[:, i, :], OA[:, i, :, :].rearrange("p h d -> p (h d)"), ACT.Square).then_inc(osq, 1)
                act.wait_ge(on_sum, 4 * (l + 1))
                act.activation(SS[:, 1, :], SS[:, 1, :], ACT.Sqrt, bias=CST[:, C_EPS + 1:C_EPS + 2],
                               scale=1.0 / HD).then_inc(on_sqrt, 1)
                for k in range(DC):
                    g = VCOL[:, 8 + 8 * l + O_ORDER[k]:8 + 8 * l + O_ORDER[k] + 1]
                    te_scale(act, TE["o", l] + k, 0, k, T, g)
                for n in range(30, 32):
                    round_unit(act, b + n, 0)
                ln_act(act, 2 * l)
                for k in range(DC):
                    te_scale(act, TE["h2", l] + k, 0, k, T, scale_col(l, 1, k), shift_col(l, 1, k))
                if l == 0:
                    act.wait_ge(zero_done, 1)
                    for q in range(4):
                        rows = ybuf.rearrange("(q p r) d -> q p (r d)", q=4, p=P)[q].rearrange("p (r d) -> p r d", d=512)
                        act.dma_start(rows, ZERO[:, :].bitcast(fp32).unsqueeze(1).to_broadcast([P, 16, 512])
                                       ).then_inc(y_st, 16)
                    swi_act(act, Swi(SWI_BASE[0], FFN_G, 0, 0), T)
            act.activation(RWH[:, :, :], RW[:, :, :], ACT.Copy).then_inc(sem("router_rounded"), 1)
            act.wait_ge(sem("route_diff"), 1)
            act.activation(RT1[:, 5, :], RT1[:, 4, :], ACT.Exp).then_inc(sem("route_exp"), 1)
            act.wait_ge(routed, 2)
            act.wait_ge(y_st, CLEARED)

            def body(sw, e, N):
                for k in range(DC):
                    te_scale(act, TE_X + k, DC * e, k % 4, N, scale_col(1, 1, k), shift_col(1, 1, k))
                blocks = (N + P - 1) // P
                (narrow_act if N == P else swi_act)(*((act, sw) if N == P else (act, sw, N)))
                for sb in range(blocks):
                    if N == P:
                        act.wait_ge(unit_used, used_at(sw.last(1)))
                    else:
                        act.wait_ge(y_t, 4 * e + sb + 1)
                    if sb == 0:
                        act.wait_ge(y_st, CLEARED + 16 * e)
                    ins = act.copy(YT[:, sb, 0:512], PS[:, 4 + sb % 2 * 2, :])
                    ins.then_inc(y_out, 1 if sb < blocks - 1 else 5 - blocks)
                act.wait_ge(sem("y_out_dve"), 4 * e + 8)
                act.wait_ge(y_out, 4 * e + 8)
                yv = ybuf.rearrange("(b p) d -> p b d", p=P)
                act.dma_start(yv[:, ds(4 * e, blocks), :], YT[:, 0:blocks, :]).then_inc(y_st, 16)
            expert(act, body)
            ln_act(act, 3)
            act.wait_ge(y_st, CLEARED + 16 * NE)

        @block.vector
        def _(dv):
            def link(ins):
                steps["dve"] += 1
                ins.then_inc(dve, 1)
                dv.wait_ge(dve, steps["dve"])

            dv.memset(ZERO[:, :].bitcast(fp32), 0.0).then_inc(zero_done, 1)
            dv.sem_inc(dtaken, DC)
            dv.wait_ge(vcol, 1)
            mod_sum(dv, 0)
            mod_sum(dv, 1)
            mod_take(dv, 0, 4)
            mod_take(dv, 1, 6)
            for l in range(NL):
                b = BASE[l]
                if l:
                    for n in range(4):
                        rest_unit(dv, b + n, 0)
                    ln_dve(dv, 1, lambda i: PS[:, 2 * i:2 * i + 2, :], lambda i: dv.wait_ge(sem("ffn_t"), i + 1))
                for k in range(DC):
                    te_split(dv, TE["h1", l] + k, 0, k, T)
                for c in range(5):
                    for u in range(4):
                        if l == 0 or c:
                            rest_unit(dv, b + 4 * c + u, 0, 2 * win_cols(c))
                    for q in MOD_WHEN[l, c]:
                        mod_sum(dv, q)
                    for j, q in enumerate(MOD_WHEN[l, c]):
                        mod_take(dv, q, mod_bank(c, j))
                dv.wait_ge(z_out, 20 * (l + 1))
                fg = [FG[:, j, :].rearrange("p (i h) -> p i h", h=HEADS) for j in range(4)]
                link(dv.tensor_tensor(fg[0], ZR[:, :, ZF:ZF + HEADS], BF[:, l:l + 1, :].to_broadcast([P, TC, HEADS]), ADD))
                link(dv.tensor_scalar(FG[:, 1, :], FG[:, 0, :], -1.0, None, MUL))
                dv.tensor_tensor(FG[:, 1, :], FG[:, 0, :], FG[:, 1, :], MIN).then_inc(gate_n, 1)
                dv.wait_ge(gate_l, 2 * (l + 1))
                dv.scalar_tensor_tensor(out=FG[:, 3, :], in0=FG[:, 0, :], scalar=0.0, in1=FG[:, 2, :],
                                        op0=MIN, op1=SUB).then_inc(gate_f, 1)
                cos, sin = (CST[:, o:o + 64].rearrange("p (i d) -> p i d", d=16) for o in (C_COS, C_SIN))
                x1, x2 = ZR[:, :, ZR_:ZR_ + 16], ZR[:, :, ZR_ + 16:ZR_ + 32]
                r = [RT8[:, j, :].rearrange("p (i d) -> p i d", d=8) for j in range(8)]
                kt = [RTK[:, j, :].rearrange("p (i d) -> p i d", d=16) for j in range(4)]
                dv.tensor_tensor(kt[0], x1, cos, MUL)
                dv.tensor_tensor(kt[1], x2, sin, MUL)
                dv.tensor_tensor(kt[2], x2, cos, MUL)
                link(dv.tensor_tensor(kt[3], x1, sin, MUL))
                dv.tensor_tensor(KRO[:, :, 0:16], kt[0], kt[1], SUB)
                dv.tensor_tensor(KRO[:, :, 16:32], kt[2], kt[3], ADD).then_inc(kr_done, 1)
                dv.wait_ge(rstd_s, l + 1)
                link(dv.reciprocal(SS[:, 0, 0:8], SS[:, 0, 0:8]))
                cn = CN[:, :, :].rearrange("p i (w c) -> p i w c", w=2)
                dv.tensor_tensor(cn, ZR[:, :, ZQ:ZQ + 512].rearrange("p i (w c) -> p i w c", w=2),
                                 SS[:, 0, 0:8].rearrange("p (i w) -> p i w", w=2).unsqueeze(3).to_broadcast([P, TC, 2, 256]),
                                 MUL).then_inc(kr_done, 1)
                dv.wait_ge(gate_s, l + 1)
                f = PS[:, 0, 0:TC * HEADS].rearrange("p (i h) -> p h i", h=HEADS)
                dv.tensor_scalar(QA[:, :, :, HD], f, 1.0, None, MUL).then_inc(gate_q, 1)
                dv.tensor_scalar(KA[:, :, :, HD + 1], f, -1.0, None, MUL).then_inc(gate_q, 1)
                for k in range(4):
                    te_split(dv, TE["c", l] + k, 0, k, T)
                for j in range(4):
                    rest_unit(dv, b + 20 + j, 0, 2 * UP_COLS[j])
                att_dve(dv, l, 0)
                dv.wait_ge(up_out, 16 * l + 8)
                q1, q2 = QA[:, :, :, 64:80], QA[:, :, :, 80:96]
                cb, sb_ = (z.unsqueeze(1).to_broadcast([P, HEADS, TC, 16]) for z in (cos, sin))
                rt = [RTMP[:, j, :].rearrange("p (h i d) -> p h i d", h=HEADS, d=16) for j in range(4)]
                dv.tensor_tensor(rt[0], q1, cb, MUL)
                dv.tensor_tensor(rt[1], q2, sb_, MUL)
                dv.tensor_tensor(rt[2], q2, cb, MUL)
                link(dv.tensor_tensor(rt[3], q1, sb_, MUL))
                dv.tensor_tensor(q1, rt[0], rt[1], SUB).then_inc(rope_done, 1)
                dv.tensor_tensor(q2, rt[2], rt[3], ADD).then_inc(rope_done, 1)
                dv.wait_ge(A["staged"], ATT(l, 1))
                dv.tensor_copy(KA[:, :, :, 64:96], KRO[:, :, :].unsqueeze(1).to_broadcast([P, HEADS, TC, ROPE])).then_inc(rope_done, 1)
                for n in range(24, 30):
                    rest_unit(dv, b + n, 0)
                att_dve(dv, l, 1)
                for i in range(TC):
                    dv.wait_ge(osq, 4 * l + i + 1)
                    dv.tensor_reduce(SS[:, 1, 16 * i:16 * i + 16], OSQ[:, i, :].rearrange("p (h d) -> p h d", d=HD),
                                     AX.X, ADD).then_inc(on_sum, 1)
                dv.wait_ge(on_sqrt, l + 1)
                dv.reciprocal(SS[:, 1, :], SS[:, 1, :]).then_inc(on_rd, 1)
                dv.wait_ge(on_rd, l + 1)
                for i in range(TC):
                    dv.tensor_tensor(OA[:, i, :, :], OA[:, i, :, :],
                                     SS[:, 1, 16 * i:16 * i + 16].unsqueeze(2).to_broadcast([P, 16, HD]), MUL).then_inc(on_done, 1)
                for k in range(DC):
                    te_split(dv, TE["o", l] + k, 0, k, T)
                for n in range(30, 32):
                    rest_unit(dv, b + n, 0)
                ln_dve(dv, 2 * l, lambda i: PS[:, i::4, :], lambda i: dv.wait_ge(unit_used, b + PER_LAYER))
                for k in range(DC):
                    te_split(dv, TE["h2", l] + k, 0, k, T)
                if l == 0:
                    swi_dve(dv, Swi(SWI_BASE[0], FFN_G, 0, 0), T)
            dv.wait_ge(sem("router_rounded"), 1)
            dv.tensor_tensor(RWL[:, :, :], RW[:, :, :], RWH[:, :, :].bitcast(fp32), SUB).then_inc(sem("router_split"), 1)
            v8 = [RT8[:, j, :].rearrange("p (i e) -> p i e", e=NE) for j in range(10)]
            v1 = [RT1[:, j, :] for j in range(8)]

            def b1(j):
                return RT1[:, j, :].unsqueeze(2).to_broadcast([P, TC, NE])
            rev = CST[:, C_REV:C_REV + NE].unsqueeze(1).to_broadcast([P, TC, NE])
            row0 = CST[:, C_ROW:C_ROW + NE].unsqueeze(1).to_broadcast([P, TC, NE])
            dv.wait_ge(sem("logits"), 1)
            link(dv.tensor_copy(RT8[:, 0, :], PS[:, 0, 0:TC * NE]))
            for c in range(2):
                link(dv.tensor_reduce(v1[c], v8[0], AX.X, MAX))
                link(dv.tensor_tensor(v8[1], v8[0], b1(c), ALU.is_equal))
                link(dv.tensor_tensor(v8[1], v8[1], rev, MUL))
                link(dv.tensor_reduce(v1[2], v8[1], AX.X, MAX))
                link(dv.tensor_tensor(v8[3 + c], b1(2), rev, ALU.is_equal))
                if c == 0:
                    link(dv.scalar_tensor_tensor(out=RT8[:, 0, :], in0=RT8[:, 3, :], scalar=-3.0 * BIG, in1=RT8[:, 0, :],
                                                 op0=MUL, op1=ADD))
            dv.tensor_tensor(v1[4], v1[1], v1[0], SUB).then_inc(sem("route_diff"), 1)
            dv.tensor_tensor(RT8[:, 5, :], RT8[:, 3, :], RT8[:, 4, :], ADD).then_inc(sem("chosen"), 1)
            dv.wait_ge(sem("route_exp"), 1)
            link(dv.tensor_scalar(v1[6], v1[5], 1.0, None, ADD))
            link(dv.reciprocal(v1[6], v1[6]))
            link(dv.tensor_tensor(v1[7], v1[5], v1[6], MUL))
            dv.wait_ge(sem("places"), 1)
            dv.tensor_copy(CNT[:, :], PS[:, 1, 32:40]).then_inc(routed, 1)
            link(dv.tensor_copy(RT8[:, 6, :], PS[:, 1, 0:32]))
            link(dv.scalar_tensor_tensor(out=RT8[:, 7, :], in0=RT8[:, 6, :], scalar=1.0, in1=RT8[:, 5, :], op0=ADD, op1=MUL))
            link(dv.tensor_scalar(RT8[:, 7, :], RT8[:, 7, :], -1.0, None, ADD))
            link(dv.tensor_tensor(v8[6], v8[6], row0, ADD))
            for c in range(2):
                link(dv.tensor_tensor(RT8[:, 8, :], RT8[:, 6, :], RT8[:, 3 + c, :], MUL))
                link(dv.tensor_reduce(v1[2], v8[8], AX.X, ADD))
                link(dv.tensor_copy(ROWI[:, c, :], v1[2]))
            link(dv.tensor_copy(XH[:, :, :], X[:, :, :]))
            link(dv.tensor_tensor(XL[:, :, :], X[:, :, :], XH[:, :, :].bitcast(fp32), SUB))
            dv.sem_inc(routed, 1)
            iota = CST[:, C_IOTA:C_IOTA + T]

            def body(sw, e, N):
                for i in range(TC):
                    ins = dv.tensor_scalar(SEL[:, i, 0:N], iota[:, 0:N], v8[7][:, i, ds(e, 1)], None, ALU.is_equal)
                ins.then_inc(sel_done, 1)
                for k in range(DC):
                    te_split(dv, TE_X + k, DC * e, k, N)
                blocks = (N + P - 1) // P
                (narrow_dve if N == P else swi_dve)(*((dv, sw) if N == P else (dv, sw, N)))
                for sb in range(blocks):
                    if N == P:
                        dv.wait_ge(unit_used, used_at(sw.last(1)))
                    else:
                        dv.wait_ge(y_t, 4 * e + sb + 1)
                    if sb == 0:
                        dv.wait_ge(y_st, CLEARED + 16 * e)
                    ins = dv.tensor_copy(YT[:, sb, 512:1024], PS[:, 5 + sb % 2 * 2, :])
                    ins.then_inc(sem("y_out_dve"), 1 if sb < blocks - 1 else 5 - blocks)
            dv.memset(ACC[:, :, :], 0.0).then_inc(sem("y_out_dve"), 4)
            dv.wait_ge(sem("y_out_dve"), 4)
            expert(dv, body)
            link(dv.tensor_tensor(X[:, :, :], XH[:, :, :].bitcast(fp32), XL[:, :, :].bitcast(fp32), ADD))

            def ready(i):
                dv.wait_ge(sem(f"y_back{i % 2}"), 32 * (i // 2 + 1))
                y0, y1 = YG[i % 2]
                link(dv.tensor_scalar(y0[:, :], y0[:, :], RT1[:, 6, i:i + 1], None, MUL))
                link(dv.scalar_tensor_tensor(out=y0[:, :], in0=y1[:, :], scalar=RT1[:, 7, i:i + 1], in1=y0[:, :],
                                             op0=MUL, op1=ADD))
            ln_dve(dv, 3, lambda i: YG[i % 2][0][:, :].rearrange("p (a b) -> p a b", a=2), ready)

        @block.tensor
        def _(pe):
            pe.wait_ge(loads, 16 * 9)
            pe.transpose(PS[:, 0, 0:32], VROW[:, :], CST[0:32, C_ID:C_ID + 32]).then_inc(vrow_t, 1)
            mod_reduce(pe, 0, 4)
            mod_reduce(pe, 1, 6)
            pe.wait_ge(mod_out, 2)
            for l in range(NL):
                b = BASE[l]
                if l:
                    pe.wait_ge(acc_done, 1)
                    for i in range(TC):
                        for k in range(DC):
                            ins = pe.transpose(PS[:, 2 * i + k // 4, k % 4 * P:(k % 4 + 1) * P],
                                               ACC[:, k, i * P:(i + 1) * P], ident)
                        ins.then_inc(sem("ffn_t"), 1)
                    pe.wait_ge(ln_x, 8)
                for k in range(DC):
                    te_transposes(pe, TE["h1", l] + k, k, [X[:, i, k * P:(k + 1) * P] for i in range(TC)])
                pe.wait_ge(te_l, TE["h1", l] + 8)
                for c in range(5):
                    n = win_cols(c)
                    for u in range(4):
                        pe.wait_ge(split, b + 4 * c + u + 1)
                        s = (b + 4 * c + u) % RING
                        for i in range(TC):
                            if u == 0 and c >= 2:
                                pe.wait_ge(z_out, 20 * l + 4 * (c - 2) + i + 1)
                            if u == 0 and i == 2 and c:
                                pe.wait_ge(mod_out, MOD_WHEN[l, c - 1][-1] + 1)
                            for kk in range(2):
                                k = 2 * u + kk
                                for j, (ht, wt) in enumerate(((HTH, WH), (HTH, WL), (HTL, WH))):
                                    ins = pe.matmul(PS[:, c % 2 * 4 + i, 0:n], ht[:, k, i * P:(i + 1) * P],
                                                    wt[s][:, kk * n:(kk + 1) * n],
                                                    start=(k == 0 and j == 0), stop=(k == DC - 1 and j == 2))
                        ins.then_inc(unit_used, 1)
                    for j, q in enumerate(MOD_WHEN[l, c]):
                        if c:
                            pe.wait_ge(z_out, 20 * l + 4 * c)
                        mod_reduce(pe, q, mod_bank(c, j))
                pe.wait_ge(z_out, 20 * (l + 1))
                if l == 0:
                    pe.wait_ge(mod_out, 8)
                pe.wait_ge(gate_f, l + 1)
                for i in range(TC):
                    for j in range(i + 1):
                        w = CST[:, C_TRI:C_TRI + P] if j == i else ones
                        ins = pe.matmul(PS[:, 0, i * HEADS:(i + 1) * HEADS], w, FG[:, 3, j * HEADS:(j + 1) * HEADS],
                                        start=(j == 0), stop=(j == i))
                ins.then_inc(gate_s, 1)
                pe.wait_ge(kr_done, 2 * (l + 1))
                for k in range(4):
                    te_transposes(pe, TE["c", l] + k, 4 + k, [CN[:, i, k * P:(k + 1) * P] for i in range(TC)])
                att_pe(pe, l, 0)
                pe.wait_ge(A["oev"], ATT(l, 1))
                for j in range(4):
                    n = UP_COLS[j]
                    s = (b + 20 + j) % RING
                    pe.wait_ge(split, b + 20 + j + 1)
                    k0 = 0 if j < 2 else 2
                    for i in range(TC):
                        if j >= 2:
                            pe.wait_ge(up_out, 16 * l + 4 * (j - 2) + i + 1)
                        for kk in range(2):
                            for z, (ht, wt) in enumerate(((HTH, WH), (HTH, WL), (HTL, WH))):
                                ins = pe.matmul(PS[:, j % 2 * 4 + i, 0:n], ht[:, k0 + kk, i * P:(i + 1) * P],
                                                wt[s][:, kk * n:(kk + 1) * n],
                                                start=(kk == 0 and z == 0), stop=(kk == 1 and z == 2))
                    ins.then_inc(unit_used, 1)
                att_pe(pe, l, 1)
                pe.wait_ge(A["oev"], ATT(l, 1) + HEADS)
                pe.wait_ge(on_done, 4 * (l + 1))
                for k in range(DC):
                    te_transposes(pe, TE["o", l] + k, k,
                                  [OA[:, i, 2 * k:2 * k + 2, :].rearrange("p h d -> p (h d)") for i in range(TC)])
                pe.wait_ge(te_l, TE["o", l] + 8)
                for half in range(2):
                    for u in range(4):
                        n = b + 24 + 4 * half + u
                        pe.wait_ge(split, n + 1)
                        for i in range(TC):
                            for kk in range(2):
                                k = 2 * u + kk
                                for j, (ht, wt) in enumerate(((HTH, WH), (HTH, WL), (HTL, WH))):
                                    ins = pe.matmul(PS[:, 4 * half + i, :], ht[:, k, i * P:(i + 1) * P],
                                                    wt[n % RING][:, kk * 512:(kk + 1) * 512],
                                                    start=(k == 0 and j == 0), stop=(k == DC - 1 and j == 2))
                        ins.then_inc(unit_used, 1)
                pe.wait_ge(ln_x, 8 * l + 4)
                for k in range(DC):
                    te_transposes(pe, TE["h2", l] + k, k, [X[:, i, k * P:(k + 1) * P] for i in range(TC)])
                pe.wait_ge(te_l, TE["h2", l] + 8)
                if l == 0:
                    swi_pe(pe, Swi(SWI_BASE[0], FFN_G, 0, 0), T)
            pe.wait_ge(sem("router_split"), 1)
            for i in range(TC):
                for k in range(DC):
                    for j, (ht, wt) in enumerate(((HTH, RWH), (HTH, RWL), (HTL, RWH))):
                        ins = pe.matmul(PS[:, 0, i * NE:(i + 1) * NE], ht[:, k, i * P:(i + 1) * P], wt[:, k, :],
                                        start=(k == 0 and j == 0), stop=(k == DC - 1 and j == 2))
            ins.then_inc(sem("logits"), 1)
            pe.wait_ge(sem("chosen"), 1)
            for i in range(TC + 1):
                for j in range(min(i + 1, TC)):
                    w = CST[:, C_STRI:C_STRI + P] if j == i else ones
                    ins = pe.matmul(PS[:, 1, i * NE:(i + 1) * NE], w, RT8[:, 5, j * NE:(j + 1) * NE],
                                    start=(j == 0), stop=(j == min(i, TC - 1)))
            ins.then_inc(sem("places"), 1)
            pe.wait_ge(zero_done, 1)
            pe.wait_ge(routed, 2)

            def body(sw, e, N):
                pe.wait_ge(sel_done, e + 1)
                for k in range(DC):
                    if k >= 4:
                        pe.wait_ge(te_a, TE_X + DC * e + k - 3)
                    for i in range(TC):
                        for j, xt in enumerate((XH, XL)):
                            ins = pe.matmul(PS[:, k % 4, 0:N], xt[:, i, k * P:(k + 1) * P], SEL[:, i, 0:N],
                                            start=(i == 0 and j == 0), stop=(i == TC - 1 and j == 1))
                    ins.then_inc(te_t, 1)
                if N > P:
                    pe.sem_inc(ht_done, EXP_G)
                pe.wait_ge(y_out, 4 * e + 4)
                pe.wait_ge(sem("y_out_dve"), 4 * e + 4)
                pe.wait_ge(te_l, TE_X + DC * e + DC)
                if N == P:
                    narrow_pe(pe, sw)
                    return
                swi_pe(pe, sw, N)
                pe.wait_ge(acc_done, e + 2)
                blocks = (N + P - 1) // P
                for sb in range(blocks):
                    if sb >= 2:
                        pe.wait_ge(y_out, 4 * e + sb + 3)
                        pe.wait_ge(sem("y_out_dve"), 4 * e + sb + 3)
                    for k in range(DC):
                        ins = pe.transpose(PS[:, 4 + sb % 2 * 2 + k // 4, k % 4 * P:(k % 4 + 1) * P],
                                           ACC[:, k, sb * P:(sb + 1) * P], ident)
                    ins.then_inc(y_t, 1 if sb < blocks - 1 else 5 - blocks)
            expert(pe, body)


_NAMES = ['x', 'c', 'w_mod', 'b_mod', 'w_in', 'b_fgate', 'w_conv', 'q_norm_g', 'kv_norm_g', 'w_uq', 'w_ukv',
          'head_norm_g', 'w_o', 'ln1_g', 'ln1_b', 'ln2_g', 'ln2_b', 'ffn_w_gate', 'ffn_w_up', 'ffn_w_down',
          'router_w', 'exp_w_gate', 'exp_w_up', 'exp_w_down']


def constants():
    import numpy as np
    c = np.zeros((P, C_W), np.float32)
    r = np.arange(P)
    c[:, C_ID:C_ID + P] = np.eye(P)
    c[:, C_ONE:C_ONE + P] = 1
    c[:, C_TRI:C_TRI + P] = r[:, None] <= r[None, :]
    c[:, C_STRI:C_STRI + P] = r[:, None] < r[None, :]
    c[:, C_MASK:C_MASK + P] = np.where(r[None, :] <= r[:, None], 0, -BIG)
    pos = (r[:, None] + P * np.arange(TC)[None, :]).astype(np.float32)
    inv = (np.float32(10000.0) ** (-np.arange(0, ROPE, 2, dtype=np.float32) / np.float32(ROPE))).astype(np.float32)
    ang = pos[:, :, None] * inv[None, None, :]
    c[:, C_COS:C_COS + 64] = np.cos(ang).reshape(P, 64)
    c[:, C_SIN:C_SIN + 64] = np.sin(ang).reshape(P, 64)
    c[:, C_IOTA:C_IOTA + T] = np.arange(T)
    c[:, C_REV:C_REV + NE] = NE - np.arange(NE)
    c[:, C_ROW:C_ROW + NE] = T * np.arange(NE)
    c[:, C_EPS], c[:, C_EPS + 1] = EPS_LN, EPS_RMS
    return c


def kernel(**inputs):
    import numpy as np
    import concourse.bacc as bacc
    from concourse import mybir as mb
    from concourse.bass_utils import run_bass_kernel_spmd as run

    nc = bacc.Bacc("TRN2", target_bir_lowering=False, num_devices=1)
    arrays, aps = {}, {}
    for name in _NAMES + ["consts"]:
        v = np.ascontiguousarray(inputs[name]) if name != "consts" else constants()
        arrays["in_" + name] = v
        aps[name] = nc.dram_tensor("in_" + name, v.shape, mb.dt.from_np(v.dtype), kind="ExternalInput").ap()
    out = nc.dram_tensor("out", (1, T, D), mb.dt.float32, kind="ExternalOutput").ap()
    ybuf = nc.dram_tensor("expert_rows", (NE * T, D), mb.dt.float32, kind="Internal").ap()
    program(nc, aps, out, ybuf)
    return run(nc, [arrays], core_ids=[0]).results[0]["out"]
```

```python
import concourse.bass as bass
from concourse import mybir
from contextlib import ExitStack

P = 128
T, D = 512, 1024
TC, DC = T // P, D // P
NL = 2
HEADS, HD = 6, 64
KQ_MLA = 96
ROPE = 32
IN_W = 2470
FF, FE, NE = 2816, 3584, 8
EPS_LN, EPS_RMS = 1e-5, 1e-6
ALPHA = (2 * NL) ** 0.25
BIG = 1e30
Z0 = 3 * HEADS * HD
ZF, ZB, ZC, ZH, ZQ, ZK, ZR_ = 0, 6, 262, 518, 774, 1030, 1286
ZW = IN_W - Z0
C_ID, C_ONE, C_TRI, C_STRI, C_MASK, C_COS, C_SIN, C_IOTA, C_REV, C_ROW, C_EPS = (
    0, 128, 256, 384, 512, 640, 704, 768, 1280, 1288, 1296)
C_W = 1300
RING = 6
UNIT = 1024
PER_LAYER = 20 + 4 + 8
FFN_G, EXP_G = FF // 256, FE // 256
BASE = [0, PER_LAYER + 6 * FFN_G]
SWI_BASE = [PER_LAYER, BASE[1] + PER_LAYER]
WIDTHS = [P, 192, 224, 256, 320, 384, 448, 512]
O_CHUNKS = [slice(0, 2), slice(2, 6, 3), slice(6, 8), slice(3, 5)]
O_ORDER = [0, 1, 2, 5, 6, 7, 3, 4]


def program(nc, a, out, ybuf):
    fp32, f32r, i32, u32 = mybir.dt.float32, mybir.dt.float32r, mybir.dt.int32, mybir.dt.uint32
    ACT, ALU, AX = mybir.ActivationFunctionType, mybir.AluOpType, mybir.AxisListType
    ds = bass.ds
    MUL, ADD, SUB, MAX, MIN = ALU.mult, ALU.add, ALU.subtract, ALU.max, ALU.min
    ctx = ExitStack()
    with ctx:
        start = (nc.sbuf_base + 31) // 32 * 32
        used = [start]

        def at(name, shape, dt, offset=None):
            size = 4
            for n in shape[1:]:
                size *= n
            if offset is None:
                offset = used[0]
                used[0] += (size + 31) // 32 * 32
            return nc.alloc_sbuf_tensor_at(name, shape, dt, offset=offset)

        sems = {}

        def sem(name):
            if name not in sems:
                sems[name] = ctx.enter_context(nc.semaphore(name))
            return sems[name]

        X = at("X", [P, TC, D], fp32)
        XL = at("XL", [P, TC, D], f32r, start)
        HTH = at("HTH", [P, DC, T], f32r)
        hth_at = start + 16384
        HTL = at("HTL", [P, DC, T], f32r)
        htl_at = hth_at + 16384
        RAW = [at(f"RAW{i}", [P, UNIT], fp32) for i in range(RING)]
        WH = [at(f"WH{i}", [P, UNIT], f32r) for i in range(RING)]
        WL = [at(f"WL{i}", [P, UNIT], f32r) for i in range(RING)]
        CST = at("CST", [P, C_W], fp32)
        TMP = at("TMP", [P, 2, T], fp32)
        xg_at = used[0]
        GB = at("GB", [P, 2, D], fp32)
        XG = [at("XG0", [P, D], fp32, xg_at)]
        ident = CST[:, C_ID:C_ID + P]
        ones = CST[:, C_ONE:C_ONE + P]
        VROW = at("VROW", [32, P], fp32)
        CACT = at("CACT", [P, DC], fp32)
        VCOL = at("VCOL", [P, 24], fp32)
        NCOL = at("NCOL", [P, 4 * NL * DC], fp32)
        NMC = at("NMC", [P, 3, 2, DC], fp32)
        MODC = at("MODC", [P, 2 * NL * 2, DC], fp32)
        BF = at("BF", [P, NL, HEADS], fp32)
        sel_at = used[0]
        FG = at("FG", [P, 4, TC * HEADS], fp32)
        SS = at("SS", [P, 2, 64], fp32)
        KRO = at("KRO", [P, TC, ROPE], fp32)
        RTK = at("RTK", [P, 4, 64], fp32)
        SEL = [at("SEL0", [P, TC, P], f32r, sel_at)]
        assert used[0] - sel_at >= 4 * TC * P
        NM = at("NM", [P, 2, TC], fp32)
        RSUM = at("RSUM", [P, 2, TC], fp32)
        RD = at("RD", [P, 2, TC], fp32)
        BNS = at("BNS", [P, 2, 12], fp32)
        MV = at("MV", [P, 2, 2], fp32)
        LNS = at("LNS", [P, 2, 2], fp32)
        RW = at("RW", [P, DC, NE], fp32)
        RWH = at("RWH", [P, DC, NE], f32r)
        RWL = at("RWL", [P, DC, NE], f32r)
        RT8 = at("RT8", [P, 10, TC * NE], fp32)
        RT1 = at("RT1", [P, 8, TC], fp32)
        PLACE = at("PLACE", [P, TC, NE + 1], fp32)
        CNT = at("CNT", [P, NE], i32)
        ROWI = at("ROWI", [P, 2, TC], u32)
        ZERO = at("ZERO", [P, 512], f32r)
        arena = used[0]
        QA = at("QA", [P, HEADS, TC, KQ_MLA], fp32)
        KA = at("KA", [P, HEADS, TC, KQ_MLA], fp32)
        VA = at("VA", [P, HEADS, TC, HD], fp32)
        zr_at = used[0]
        ZR = at("ZR", [P, TC, ZW], fp32)
        oa_at = used[0]
        OA = at("OA", [P, TC, 16, HD], fp32)
        assert used[0] <= nc.sbuf_usable_end, (used[0], nc.sbuf_usable_end)
        MACC = [at(f"MACC{i}", [P, D], fp32, oa_at + 4096 * i) for i in range(2)]
        MODW = [at(f"MODW{i}", [P, D], fp32, oa_at + 4096 * (2 + i)) for i in range(2)]
        NROW = at("NROW", [4 * NL * DC, P], fp32, zr_at)
        CN = at("CN", [P, TC, 512], fp32, htl_at + 8192)
        U1 = at("U1", [P, TC, 256], fp32, oa_at)
        U2 = at("U2", [P, TC, 256], fp32, oa_at + 4096)
        QT = [at(f"QT{i}", [P, T], fp32, hth_at + 8192 + 2048 * i) for i in range(2)]
        KT = [at(f"KT{i}", [P, T], fp32, hth_at + 12288 + 2048 * i) for i in range(2)]
        SQ = [at(f"SQ{i}", [P, TC, KQ_MLA], fp32, zr_at + 3072 * i) for i in range(2)]
        SK = [at(f"SK{i}", [P, TC, KQ_MLA], fp32, zr_at + 3072 * i + 1536) for i in range(2)]
        PR = [at(f"PR{i}", [P, T], fp32, zr_at + 6144 + 2048 * i) for i in range(2)]
        PTS = [at(f"PTS{i}", [P, T], fp32, zr_at + 10240 + 2048 * i) for i in range(2)]
        RTMP = at("RTMP", [P, 4, HEADS * TC * 16], fp32, zr_at + 14336)
        WCV = at("WCV", [P, 3, 256], fp32, oa_at + 8192)
        OSQ = at("OSQ", [P, TC, D], fp32, arena)
        ACC = at("ACC", [P, DC, T], fp32, arena)
        HAH = at("HAH", [P, 2, T], f32r, arena + 16384)
        HAL = at("HAL", [P, 2, T], f32r, arena + 20480)
        SIL = at("SIL", [P, 2, T], fp32, arena + 24576)
        XG.append(at("XG1", [P, D], fp32, arena + 16384))
        SEL.append(at("SEL1", [P, TC, P], f32r, arena + 20480))
        LT = [at(f"LT{i}", [P, D], fp32, arena + 16384 + 4096 * i) for i in range(2)]
        LNR = at("LNR", [P, 2, D], fp32, arena + 28672)
        YT = at("YT", [P, TC, D], fp32, arena + 28672)
        XH = at("XH", [P, TC, D], f32r, arena + 45056)
        YG = [[at(f"YG{i}{j}", [P, D], fp32, (arena if i < 2 else hth_at) + 8192 * (i % 2) + 4096 * j) for j in range(2)]
              for i in range(TC)]
        assert arena + 45056 + 16384 <= nc.sbuf_usable_end
        PS = ctx.enter_context(nc.psum_tensor("PS", [P, 8, 512], fp32))

        w_in = a["w_in"].rearrange("l (k p) n -> l p k n", p=P)
        w_mod = a["w_mod"].rearrange("l (k p) n -> l p k n", p=P)
        w_uq = a["w_uq"].rearrange("l (k p) n -> l p k n", p=P)
        w_ukv = a["w_ukv"].rearrange("l (k p) n -> l p k n", p=P)
        w_o = a["w_o"].rearrange("l (k p) n -> l p k n", p=P)
        x_d = a["x"].rearrange("b (i p) d -> p (b i) d", p=P)
        out_d = out.rearrange("b (i p) d -> p (b i) d", p=P)
        up_w = [[a["ffn_w_gate"], a["ffn_w_up"]], [a["exp_w_gate"][0], a["exp_w_up"][0]]]
        up_w = [[w.rearrange("e (k p) f -> p (e k) f", p=P) for w in pair] for pair in up_w]
        dn_w = [a["ffn_w_down"], a["exp_w_down"][0]]
        dn_w = [w.rearrange("e (k p) d -> p (e k) d", p=P) for w in dn_w]

        raw_ready = [sem(f"raw_ready{i}") for i in range(RING)]
        rounded, split, unit_used = sem("rounded"), sem("split"), sem("unit_used")

        def load(eng, c, d6, src, k, n):
            if c >= RING:
                eng.wait_ge(split, c - RING + 1 + RING * d6)
            dst = RAW[c % RING][:, 0:k * n].rearrange("p (k n) -> p k n", k=k)
            eng.dma_start(dst, src).then_inc(raw_ready[c % RING], 16)

        def round_unit(eng, c, d6, n=UNIT):
            s = c % RING
            eng.wait_ge(raw_ready[s], 16 * (c // RING + 1 + d6))
            if c >= RING:
                eng.wait_ge(unit_used, c - RING + 1 + RING * d6)
            eng.copy(WH[s][:, 0:n], RAW[s][:, 0:n]).then_inc(rounded, 1)

        def rest_unit(eng, c, d6, n=UNIT):
            s = c % RING
            eng.wait_ge(rounded, c + 1 + RING * d6)
            eng.tensor_tensor(WL[s][:, 0:n], RAW[s][:, 0:n], WH[s][:, 0:n].bitcast(fp32), SUB).then_inc(split, 1)

        def win_cols(c):
            return min(512, IN_W - 512 * c)

        UP_COLS = [480, 96, 512, 256]

        def unit_cols(l, n):
            if n < 20:
                return 2 * win_cols(n // 4)
            return 2 * UP_COLS[n - 20] if n < 24 else UNIT

        te_t, te_a, te_h, te_l = sem("te_transposed"), sem("te_scaled"), sem("te_rounded"), sem("te_split")
        TE = {}
        for l in range(NL):
            for j, (stage, _) in enumerate([("h1", 8), ("c", 4), ("o", 8), ("h2", 8)]):
                TE[stage, l] = 28 * l + [0, 8, 12, 20][j]
        TE_X = 28 * NL

        def te_scale(eng, m, md, bank, n, scale, bias=0.0):
            eng.wait_ge(te_t, m + 1 + md)
            if m >= 2:
                eng.wait_ge(te_l, m - 1 + md)
            eng.activation(TMP[:, m % 2, 0:n], PS[:, bank, 0:n], ACT.Identity, bias=bias, scale=scale).then_inc(te_a, 1)

        def te_split(eng, m, md, k, n):
            eng.wait_ge(te_a, m + 1 + md)
            eng.tensor_copy(HTH[:, k, 0:n], TMP[:, m % 2, 0:n]).then_inc(te_h, 1)
            eng.wait_ge(te_h, m + 1 + md)
            eng.tensor_tensor(HTL[:, k, 0:n], TMP[:, m % 2, 0:n], HTH[:, k, 0:n].bitcast(fp32), SUB).then_inc(te_l, 1)

        def te_transposes(eng, m, bank, srcs):
            for i, s in enumerate(srcs):
                ins = eng.transpose(PS[:, bank, i * P:(i + 1) * P], s, ident)
            ins.then_inc(te_t, 1)

        sel_done, gathered, xg_a, xg_v = (sem(s) for s in ("selected", "rows_gathered", "rows_out_act", "rows_out_dve"))

        def block_select(eng, e, j, first=False):
            if not first:
                eng.wait_ge(gathered, 4 * e + j - (j > 1))
            for i in range(TC):
                ins = eng.tensor_scalar(SEL[j % 2][:, i, :], CST[:, C_IOTA + j * P:C_IOTA + (j + 1) * P],
                                        PLACE[:, i, ds(e, 1)], None, ALU.is_equal)
            ins.then_inc(sel_done, 1)

        def block_gather(eng, e, j, bank):
            eng.wait_ge(sel_done, 4 * e + j + 1)
            for h in range(2):
                for i in range(TC):
                    for z, xt in enumerate((XH, XL)):
                        ins = eng.matmul(PS[:, bank + h, :], SEL[j % 2][:, i, :], xt[:, i, h * 512:(h + 1) * 512],
                                         start=(i == 0 and z == 0), stop=(i == TC - 1 and z == 1))
            ins.then_inc(gathered, 1)

        def block_rows(eng, e, j, bank, h):
            eng.wait_ge(gathered, 4 * e + j + 1)
            eng.wait_ge(te_t, TE_X + 2 * (4 * e + j - (j > 1)))
            dst, src = XG[j % 2][:, h * 512:(h + 1) * 512], PS[:, bank + h, :]
            (eng.copy(dst, src) if h == 0 else eng.tensor_copy(dst, src)).then_inc(xg_v if h else xg_a, 1)

        def block_turn(eng, e, j, bank):
            for h, done in enumerate((xg_a, xg_v)):
                eng.wait_ge(done, 4 * e + j + 1)
                for k in range(4):
                    ins = eng.transpose(PS[:, bank + h, k * P:(k + 1) * P], XG[j % 2][:, (4 * h + k) * P:(4 * h + k + 1) * P], ident)
                ins.then_inc(te_t, 1)

        def block_scale(eng, e, j, bank):
            for h in range(2):
                m = TE_X + 2 * (4 * e + j) + h
                eng.wait_ge(te_t, m + 1)
                eng.wait_ge(te_l, m - 1)
                for k in range(4):
                    ins = eng.activation(TMP[:, h, k * P:(k + 1) * P], PS[:, bank + h, k * P:(k + 1) * P], ACT.Identity,
                                         bias=shift_col(1, 1, 4 * h + k), scale=scale_col(1, 1, 4 * h + k))
                ins.then_inc(te_a, 1)

        def block_split(eng, e, j):
            for h in range(2):
                m = TE_X + 2 * (4 * e + j) + h
                hi, lo = (z[:, 4 * h:4 * h + 4, j * P:(j + 1) * P] for z in (HTH, HTL))
                t = TMP[:, h, :].rearrange("p (k n) -> p k n", n=P)
                eng.wait_ge(te_a, m + 1)
                eng.tensor_copy(hi, t).then_inc(te_h, 1)
                eng.wait_ge(te_h, m + 1)
                eng.tensor_tensor(lo, t, hi.bitcast(fp32), SUB).then_inc(te_l, 1)

        def no_blocks(eng, e, blocks, *counts):
            if blocks < 4:
                for s, base, k in counts:
                    eng.wait_ge(s, base + k * (4 * e + blocks))
                    eng.sem_inc(s, k * (4 - blocks))

        modw_ready = [sem("modw_ready0"), sem("modw_ready1")]
        mod_first = [sem(f"mod_first{i}") for i in range(RING)]
        modw_scaled = sem("modw_scaled")
        macc_init = [sem("macc_init0"), sem("macc_init1")]
        modw_used, macc_zero = sem("modw_used"), sem("macc_zero")
        mod_red, mod_out = sem("mod_reduced"), sem("mod_out")
        MOD_WHEN = {(0, 0): [2], (0, 1): [3], (0, 2): [4], (0, 3): [5], (0, 4): [],
                    (1, 0): [8], (1, 1): [9], (1, 2): [10], (1, 3): [11], (1, 4): []}

        def mod_bank(c, j):
            return ((c + 1) % 2) * 4 + (2 if c < 4 else j * 2)

        def mod_load(eng, q, part=None):
            l, s = divmod(q, 6)
            if q >= 2:
                eng.wait_ge(mod_red, q - 1)
            eng.memset(MACC[q % 2][:, :], 0.0).then_inc(macc_zero, 1)
            eng.wait_ge(macc_zero, q + 1)
            eng.dma_start(MACC[q % 2][0:1, :], a["b_mod"][l:l + 1, s * D:(s + 1) * D]).then_inc(macc_init[q % 2], 16)
            for k in range(DC if q >= 2 else 0):
                m = 8 * q + k
                eng.wait_ge(modw_used, m - 1)
                eng.dma_start(MODW[m % 2][:, :], w_mod[l, :, k, s * D:(s + 1) * D]).then_inc(modw_ready[m % 2], 16)
                if part and k:
                    part(k - 1)
            if part:
                part(DC - 1)

        def mod_load_first(eng, m):
            if m >= RING:
                eng.wait_ge(modw_used, m - RING + 1)
            q, k = divmod(m, DC)
            eng.dma_start(RAW[m % RING][:, :], w_mod[0, :, k, q * D:(q + 1) * D]).then_inc(mod_first[m % RING], 16)

        def mod_sum_pool(eng, q, k):
            if k == 0:
                eng.wait_ge(macc_init[q % 2], 16 * (q // 2 + 1))
            m = 8 * q + k
            w = MODW[m % 2][:, :]
            eng.wait_ge(modw_ready[m % 2], 16 * (m // 2 - 7))
            eng.tensor_tensor(w, w, CACT[:, k:k + 1].to_broadcast([P, D]), MUL).then_inc(modw_scaled, 1)
            eng.wait_ge(modw_scaled, m - 47)
            eng.wait_ge(modw_used, m)
            eng.tensor_tensor(MACC[q % 2][:, :], MACC[q % 2][:, :], w, ADD).then_inc(modw_used, 1)

        def mod_sum(eng, q):
            eng.wait_ge(macc_init[q % 2], 16 * (q // 2 + 1))
            for k in range(DC):
                m = 8 * q + k
                if q < 2:
                    eng.wait_ge(mod_first[m % RING], 16 * (m // RING + 1))
                else:
                    eng.wait_ge(modw_ready[m % 2], 16 * (m // 2 - 7))
                rows = RAW[m % RING] if q < 2 else MODW[m % 2]
                if m:
                    eng.wait_ge(modw_used, m)
                eng.scalar_tensor_tensor(out=MACC[q % 2][:, :], in0=rows[:, :], scalar=CACT[:, k:k + 1],
                                         in1=MACC[q % 2][:, :], op0=MUL, op1=ADD).then_inc(modw_used, 1)

        def mod_reduce(eng, q, bank):
            eng.wait_ge(modw_used, 8 * (q + 1))
            if q % 3 == 2:
                for h in range(2):
                    ins = eng.matmul(PS[:, bank + h, :], ones, MACC[q % 2][:, h * 512:(h + 1) * 512],
                                     start=True, stop=True)
            else:
                for j in range(DC):
                    ins = eng.matmul(PS[:, bank, j:j + 1], MACC[q % 2][:, j * P:(j + 1) * P], ones[:, 0:1],
                                     start=True, stop=True)
            ins.then_inc(mod_red, 1)

        def mod_take(eng, q, bank):
            l, s = divmod(q, 6)
            eng.wait_ge(mod_red, q + 1)
            if s % 3 == 2:
                ins = eng.tensor_scalar(GB[:, s // 3, :], PS[:, bank:bank + 2, :], 1.0, None, ADD)
            else:
                ins = eng.tensor_scalar(MODC[:, 4 * l + 2 * (s // 3) + s % 3, :], PS[:, bank, 0:DC],
                                        float(s % 3), None, ADD)
            ins.then_inc(mod_out, 1)

        def shift_col(l, j, k):
            return MODC[:, 4 * l + 2 * j, k:k + 1]

        def norm_cols(eng, n):
            l, w = divmod(n, 2)
            lm, j = divmod(n + 1, 2)
            gain, offset = (NCOL[:, (2 * w + z) * NL * DC + l * DC:(2 * w + z) * NL * DC + (l + 1) * DC] for z in range(2))
            scale, shift = MODC[:, 4 * lm + 2 * j + 1, :], MODC[:, 4 * lm + 2 * j, :]
            if n == 0:
                eng.wait_ge(vcol, 2)
            eng.wait_ge(mod_out, (5, 8, 11)[n])
            eng.tensor_tensor(NMC[:, n, 0, :], scale, gain, MUL).then_inc(ncol, 1)
            eng.tensor_tensor(NMC[:, n, 1, :], scale, offset, MUL).then_inc(ncol, 1)
            eng.wait_ge(ncol, 3 * n + 2)
            eng.tensor_tensor(NMC[:, n, 1, :], NMC[:, n, 1, :], shift, ADD).then_inc(ncol, 1)

        def affine(eng, n, turned=None):
            if turned:
                eng.wait_ge(te_t, turned)
            eng.wait_ge(lnr_load, 32 * (n + 1))
            if n:
                eng.wait_ge(ln_x, 4 * n)
            for i in range(TC):
                if not turned:
                    eng.wait_ge(ln_n, 4 * n + i + 1)
                eng.tensor_tensor(X[:, i, :], X[:, i, :], LNR[:, 0, :], MUL).then_inc(ln_aff, 1)
                eng.wait_ge(ln_aff, 4 * n + i + 1)
                eng.tensor_tensor(X[:, i, :], X[:, i, :], LNR[:, 1, :], ADD).then_inc(ln_x, 1)

        def scale_col(l, j, k):
            return MODC[:, 4 * l + 2 * j + 1, k:k + 1]

        loads, x_load = sem("first_loads"), sem("x_load")
        vrow_t, vcol, ncol = sem("vrow_transposed"), sem("vcol"), sem("norm_cols")
        z_out = sem("z_out")
        gate_n, gate_l, gate_f, gate_s, gate_q = (sem("gate_" + s) for s in ("neg", "log", "f", "sum", "q"))
        ssq, rstd_s, rstd, cn_done, kr_done = (sem(s) for s in ("ct_squares", "ct_sqrt", "ct_rstd", "ct_norm", "k_rope"))
        conv_done, wcv_load, uc, shifted, pool_step = (sem(s) for s in ("conv", "wconv_load", "conv_u", "conv_shifted", "pool_step"))
        up_out, rope_done = sem("up_out"), sem("roped")
        A = {s: sem("att_" + s) for s in ("staged", "tq", "tk", "qev", "kev", "score", "mask", "max", "exp", "tp", "pev", "pv", "rd", "oev")}
        osq, on_sum, on_sqrt, on_rd, on_done = (sem("on_" + s) for s in ("sq", "sum", "sqrt", "rd", "done"))
        ln_v, ln_s, ln_n, ln_x, lnr_load = (sem("ln_" + s) for s in ("var", "sqrt", "norm", "x", "rows"))
        ln_bn, ln_aff = sem("ln_bn"), sem("ln_affine")
        dve = sem("dve_step")
        steps = {"dve": 0}

        def ATT(l, g):
            return HEADS * (2 * l + g)

        def stage_head(eng, hb, h, p, K, wait):
            if wait:
                eng.wait_ge(A["tk"], hb - 1)
            eng.tensor_copy(SQ[p][:, :, 0:K], QA[:, ds(h, 1), :, 0:K])
            eng.tensor_copy(SK[p][:, :, 0:K], KA[:, ds(h, 1), :, 0:K]).then_inc(A["staged"], 1)

        def att_tq(eng, hb, p, K, first=False):
            eng.wait_ge(A["staged"], hb + 1)
            if not first:
                eng.wait_ge(A["kev"], hb)
            for i in range(TC):
                ins = eng.transpose(PS[0:K, 6, i * P:(i + 1) * P], SQ[p][:, i, 0:K], ident)
            ins.then_inc(A["tq"], 1)

        def att_tk(eng, hb, p, K):
            eng.wait_ge(A["qev"], hb + 1)
            for i in range(TC):
                ins = eng.transpose(PS[0:K, 6, i * P:(i + 1) * P], SK[p][:, i, 0:K], ident)
            ins.then_inc(A["tk"], 1)

        def att_score(eng, hb, i, p, K, first=False):
            if i == 0:
                eng.wait_ge(A["kev"], hb + 1)
            if not first:
                eng.wait_ge(A["exp"], 4 * hb - 3 + i)
            eng.matmul(PS[:, i, 0:(i + 1) * P], QT[p][0:K, i * P:(i + 1) * P], KT[p][0:K, 0:(i + 1) * P],
                       start=True, stop=True).then_inc(A["score"], 1)

        def att_tp(eng, hb, i, wait=True):
            eng.wait_ge(A["exp"], 4 * hb + i + 1)
            if wait:
                eng.wait_ge(A["pev"], 4 * hb + i - 1)
            for j in range(i + 1):
                ins = eng.transpose(PS[:, 4 + i % 2, j * P:(j + 1) * P], PR[i % 2][:, j * P:(j + 1) * P], ident)
            ins.then_inc(A["tp"], 1)

        def att_pv(eng, hb, h, i, p, wait):
            eng.wait_ge(A["pev"], 4 * hb + i + 1)
            if i == 0 and wait:
                eng.wait_ge(A["oev"], hb)
            c = p * 256 + i * HD
            for j in range(i + 1):
                ins = eng.matmul(PS[:, 7, c:c + HD], PTS[i % 2][:, j * P:(j + 1) * P], VA[:, ds(h, 1), j, :],
                                 start=(j == 0), stop=(j == i))
            ins.then_inc(A["pv"], 1)

        def att_pe(eng, l, g):
            K, b = (HD + 2, KQ_MLA)[g], ATT(l, g)

            def head(hb, h, p, last=False, first=False):
                w = not (first and b == 0)
                att_tp(eng, hb, 0, w)
                if not last:
                    att_tq(eng, hb + 1, 1 - p, K)
                att_tp(eng, hb, 1, w)
                att_pv(eng, hb, h, 0, p, w)
                if not last:
                    att_tk(eng, hb + 1, 1 - p, K)
                att_tp(eng, hb, 2)
                att_pv(eng, hb, h, 1, p, w)
                if not last:
                    att_score(eng, hb + 1, 0, 1 - p, K)
                    att_score(eng, hb + 1, 1, 1 - p, K)
                att_tp(eng, hb, 3)
                att_pv(eng, hb, h, 2, p, w)
                if not last:
                    att_score(eng, hb + 1, 2, 1 - p, K)
                    att_score(eng, hb + 1, 3, 1 - p, K)
                att_pv(eng, hb, h, 3, p, w)

            if g == 0:
                eng.wait_ge(gate_q, 2 * (l + 1))
                eng.wait_ge(te_l, TE["c", l] + 4)
            else:
                eng.wait_ge(up_out, 16 * (l + 1))
            att_tq(eng, b, 0, K, first=True)
            att_tk(eng, b, 0, K)
            for i in range(TC):
                att_score(eng, b, i, 0, K, first=(b == 0))
            head(b, 0, 0, first=True)
            with eng.Fori(0, 2) as it:
                head(b + 1 + 2 * it, 1 + 2 * it, 1)
                head(b + 2 + 2 * it, 2 + 2 * it, 0)
            head(b + 5, 5, 1, last=True)

        def att_act(eng, l, g):
            K, b = (HD + 2, KQ_MLA)[g], ATT(l, g)

            def qev(hb, p):
                eng.wait_ge(A["tq"], hb + 1)
                eng.copy(QT[p][0:K, :], PS[0:K, 6, :]).then_inc(A["qev"], 1)

            def exp(hb, i, p, wait=True):
                eng.wait_ge(A["max"], 4 * hb + i + 1)
                if wait:
                    eng.wait_ge(A["tp"], 4 * hb + i - 1)
                n = (i + 1) * P
                eng.activation(PR[i % 2][:, 0:n], PS[:, i, 0:n], ACT.Exp, bias=NM[:, p, i:i + 1],
                               accum_out=RSUM[:, p, i:i + 1]).then_inc(A["exp"], 1)

            def pev(hb, i, wait=True):
                eng.wait_ge(A["tp"], 4 * hb + i + 1)
                if wait:
                    eng.wait_ge(A["pv"], 4 * hb + i - 1)
                n = (i + 1) * P
                eng.copy(PTS[i % 2][:, 0:n], PS[:, 4 + i % 2, 0:n]).then_inc(A["pev"], 1)

            def head(hb, p, last=False, first=False):
                w = not (first and b == 0)
                exp(hb, 0, p, w)
                exp(hb, 1, p, w)
                pev(hb, 0, w)
                if not last:
                    qev(hb + 1, 1 - p)
                exp(hb, 2, p)
                pev(hb, 1, w)
                exp(hb, 3, p)
                pev(hb, 2)
                pev(hb, 3)

            qev(b, 0)
            head(b, 0, first=True)
            with eng.Fori(0, 2) as it:
                head(b + 1 + 2 * it, 1)
                head(b + 2 + 2 * it, 0)
            head(b + 5, 1, last=True)

        def att_dve(eng, l, g):
            K, b = (HD + 2, KQ_MLA)[g], ATT(l, g)

            def kev(hb, p):
                eng.wait_ge(A["tk"], hb + 1)
                eng.tensor_copy(KT[p][0:K, :], PS[0:K, 6, :]).then_inc(A["kev"], 1)

            def soft(hb, i, p):
                eng.wait_ge(A["score"], 4 * hb + i + 1)
                diag = PS[:, i, i * P:(i + 1) * P]
                eng.tensor_tensor(diag, diag, CST[:, C_MASK:C_MASK + P], ADD).then_inc(A["mask"], 1)
                eng.wait_ge(A["mask"], 4 * hb + i + 1)
                eng.tensor_reduce(NM[:, p, i:i + 1], PS[:, i, 0:(i + 1) * P], AX.X, MAX, negate=True).then_inc(A["max"], 1)

            def take(hb, h, p):
                eng.wait_ge(A["pv"], 4 * hb + 4)
                eng.reciprocal(RD[:, p, :], RSUM[:, p, :]).then_inc(A["rd"], 1)
                eng.wait_ge(A["rd"], hb + 1)
                o = PS[:, 7, p * 256:(p + 1) * 256].rearrange("p (i d) -> p i d", d=HD)
                eng.tensor_tensor(OA[:, :, ds(h + HEADS * g, 1), :], o, RD[:, p, :].unsqueeze(2).to_broadcast([P, TC, HD]),
                                  MUL).then_inc(A["oev"], 1)

            def head(hb, h, p, last=False, first=False):
                soft(hb, 0, p)
                soft(hb, 1, p)
                soft(hb, 2, p)
                soft(hb, 3, p)
                if not first:
                    take(hb - 1, h - 1, 1 - p)
                if not last:
                    kev(hb + 1, 1 - p)

            kev(b, 0)
            head(b, 0, 0, first=True)
            with eng.Fori(0, 2) as it:
                head(b + 1 + 2 * it, 1 + 2 * it, 1)
                head(b + 2 + 2 * it, 2 + 2 * it, 0)
            head(b + 5, 5, 1, last=True)
            take(b + 5, 5, 1)

        def att_pool(eng, l, g):
            K, b = (HD + 2, KQ_MLA)[g], ATT(l, g)
            if g == 0:
                eng.wait_ge(z_out, 20 * (l + 1))
                eng.wait_ge(gate_q, 2 * (l + 1))
                eng.wait_ge(kr_done, 2 * (l + 1))
            else:
                eng.wait_ge(up_out, 16 * (l + 1))
                eng.wait_ge(rope_done, 3 * (l + 1))
            stage_head(eng, b, 0, 0, K, b > 0)
            stage_head(eng, b + 1, 1, 1, K, b > 0)
            with eng.Fori(0, 2) as it:
                stage_head(eng, b + 2 + 2 * it, 2 + 2 * it, 0, K, True)
                stage_head(eng, b + 3 + 2 * it, 3 + 2 * it, 1, K, True)

        def ln_dve(eng, n, src, ready, dst_last=None):
            def gated(i):
                m = 4 * n + i
                ready(i)
                if i >= 2:
                    eng.wait_ge(ln_bn, 5 * (m - 2) + 2)
                eng.tensor_tensor(LT[i % 2][:, :].rearrange("p (a b) -> p a b", a=2), src(i),
                                  GB[:, n % 2, :].rearrange("p (a b) -> p a b", a=2), MUL).then_inc(ln_bn, 1)

            gated(0)
            for i in range(TC):
                m = 4 * n + i
                t = LT[i % 2]
                eng.wait_ge(ln_bn, 5 * m + 1)
                eng.scalar_tensor_tensor(out=X[:, i, :], in0=X[:, i, :], scalar=ALPHA, in1=t[:, :],
                                         op0=MUL, op1=ADD).then_inc(ln_bn, 1)
                eng.wait_ge(ln_bn, 5 * m + 2)
                for h in range(2):
                    eng.bn_stats(BNS[:, i % 2, 6 * h:6 * h + 6], X[:, i, h * 512:(h + 1) * 512]).then_inc(ln_bn, 1)
                eng.wait_ge(ln_bn, 5 * m + 4)
                if i >= 2:
                    eng.wait_ge(ln_n, m - 1)
                eng.bn_aggr(MV[:, i % 2, :], BNS[:, i % 2, :]).then_inc(ln_bn, 1)
                if i + 1 < TC:
                    gated(i + 1)
                eng.wait_ge(ln_s, m + 1)
                eng.reciprocal(LNS[:, i % 2, 0:1], LNS[:, i % 2, 0:1]).then_inc(dve, 1)
                steps["dve"] += 1
                eng.wait_ge(dve, steps["dve"])
                eng.scalar_tensor_tensor(out=LNS[:, i % 2, 1:2], in0=MV[:, i % 2, 0:1], scalar=-1.0,
                                         in1=LNS[:, i % 2, 0:1], op0=MUL, op1=MUL).then_inc(ln_v, 1)

        def ln_act(eng, n, between=lambda i: None):
            for i in range(TC):
                m = 4 * n + i
                eng.wait_ge(ln_bn, 5 * m + 5)
                eng.activation(LNS[:, i % 2, 0:1], MV[:, i % 2, 1:2], ACT.Sqrt, bias=CST[:, C_EPS:C_EPS + 1]).then_inc(ln_s, 1)
                eng.wait_ge(ln_v, m + 1)
                eng.activation(X[:, i, :], X[:, i, :], ACT.Identity, bias=LNS[:, i % 2, 1:2],
                               scale=LNS[:, i % 2, 0:1]).then_inc(ln_n, 1)
                between(i)

        def ln_rows(eng, n):
            l, w = divmod(n, 2)
            if w == 0:
                eng.wait_ge(A["oev"], ATT(l, 1) + HEADS)
            elif l == 0:
                eng.wait_ge(acc_done, 1)
            else:
                eng.wait_ge(y_st, CLEARED + 16 * NE)
            if n:
                eng.wait_ge(ln_x, 4 * n)
            for j, name in enumerate((f"ln{w + 1}_g", f"ln{w + 1}_b")):
                eng.dma_start(LNR[:, j, :], a[name][l:l + 1, :].to_broadcast([P, D])).then_inc(lnr_load, 16)

        silu_done, hm_done, hh_done, hl_done = (sem(s) for s in ("silu", "h_product", "h_rounded", "h_split"))
        dpart, dtaken, acc_done = sem("down_part"), sem("down_taken"), sem("acc_done")
        y_t, y_out, y_st = sem("y_transposed"), sem("y_out"), sem("y_stored")
        CLEARED = 16 * 4
        zero_done = sem("zero_done")

        class Swi:
            def __init__(s, base, G, gb, x, e=0, ahead=0):
                s.base, s.G, s.gb, s.x, s.e, s.ahead = base, G, gb + G * e, x + e, e, ahead

            def unit(s, g, j):
                return s.base + 4 + j, s.G * s.e + g - 1

            def unit0(s, j):
                return s.base + j, s.G * s.e

            def last(s, j):
                return s.base + 4 + j, s.G * s.e + s.G - 1

        def used_at(c_d):
            c, d = c_d
            return c + 1 + RING * d

        def swi_pe(eng, sw, N, next_block=lambda sw: None):
            small = N <= 256

            def gate_up(g, units, first):
                for w in range(2):
                    for half in range(2):
                        c, d = units(2 * w + half)
                        if half == 0 and not first:
                            eng.wait_ge(hm_done if w else silu_done, sw.gb + g)
                        eng.wait_ge(split, used_at((c, d)))
                        s = c % RING
                        for fc in range(2):
                            for kk in range(4):
                                k, o = 4 * half + kk, kk * 256 + fc * P
                                for j, (wt, xt) in enumerate(((WH, HTH), (WL, HTH), (WH, HTL))):
                                    ins = eng.matmul(PS[:, 2 * w + fc, 0:N], wt[s][:, o:o + P], xt[:, k, 0:N],
                                                     start=(k == 0 and j == 0), stop=(k == DC - 1 and j == 2))
                        ins.then_inc(unit_used, 1)

            def down(g, units):
                (c0, d0), (c1, d1) = units(4), units(5)
                eng.wait_ge(hl_done, sw.gb + g + 1)
                eng.wait_ge(split, used_at((c1, d1)))
                for dc in range(DC):
                    if small:
                        o = PS[:, 4 + dc // 2, dc % 2 * 256:dc % 2 * 256 + N]
                    else:
                        eng.wait_ge(dtaken, DC * (sw.gb + g) + DC + dc - 3)
                        o = PS[:, 4 + dc % 4, 0:N]
                    for fc, c in enumerate((c0, c1)):
                        s = c % RING
                        for j, (wt, ht) in enumerate(((WH, HAH), (WL, HAH), (WH, HAL))):
                            ins = eng.matmul(o, wt[s][:, dc * P:(dc + 1) * P], ht[:, fc, 0:N],
                                             start=(not small and fc == 0 and j == 0),
                                             stop=(not small and fc == 1 and j == 2), skip_group_check=small)
                        if dc == DC - 1 and fc == 0:
                            ins.then_inc(unit_used, 1)
                    if not small and dc < DC - 1:
                        ins.then_inc(dpart, 1)
                if small:
                    ins.then_inc(unit_used, 1)
                else:
                    ins.then_inc(dpart, 1)
                    eng.wait_ge(dpart, DC * (sw.gb + g + 1))
                    eng.sem_inc(unit_used, 1)

            if small:
                for b in range(4):
                    ins = eng.matmul(PS[:, 4 + b, :], ZERO[:, 0:P], ZERO[:, :], start=True, stop=False,
                                     skip_group_check=True)
                ins.then_inc(dpart, DC * sw.G)
            gate_up(0, sw.unit0, True)
            with eng.Fori(1, sw.G) as g:
                gate_up(g, lambda j: sw.unit(g, j), False)
                down(g - 1, lambda j: sw.unit(g, j))
            next_block(sw)
            down(sw.G - 1, lambda j: sw.last(j - 4))

        def clear_acc(eng, sw, N):
            eng.memset(ACC[:, :, 0:N], 0.0).then_inc(dve_acc, 1)
            eng.wait_ge(dve_acc, sw.x + 1)

        def swi_act(eng, sw, N, next_block=lambda sw: None):
            def rounded_h(g):
                eng.wait_ge(hm_done, sw.gb + g + 1)
                eng.activation(HAH[:, :, 0:N], SIL[:, :, 0:N], ACT.Copy).then_inc(hh_done, 1)

            def body(g, first):
                for j in range(2):
                    round_unit(eng, *sw.unit(g, j))
                silu0(g - 1, first)
                for j in range(2, 4):
                    round_unit(eng, *sw.unit(g, j))
                if not first:
                    eng.wait_ge(unit_used, used_at(sw.unit(g - 1, 5)))
                rounded_h(g - 1)
                for j in range(4, 6):
                    round_unit(eng, *sw.unit(g, j))

            def silu0(g, first):
                if first:
                    eng.wait_ge(unit_used, used_at(sw.unit0(1)))
                else:
                    eng.wait_ge(hl_done, sw.gb + g)
                    eng.wait_ge(unit_used, used_at(sw.unit(g, 1)))
                eng.activation(SIL[:, :, 0:N], PS[:, 0:2, 0:N], ACT.Silu).then_inc(silu_done, 1)

            for j in range(sw.ahead, 4):
                round_unit(eng, *sw.unit0(j))
            body(1, True)
            with eng.Fori(2, sw.G) as g:
                body(g, False)
            silu0(sw.G - 1, False)
            eng.wait_ge(unit_used, used_at(sw.unit(sw.G - 1, 5)))
            rounded_h(sw.G - 1)
            for j in range(2):
                round_unit(eng, *sw.last(j))
            next_block(sw)

        def swi_dve(eng, sw, N, next_select=lambda sw: None, next_block=lambda sw: None):
            small = N <= 256

            def product(g):
                eng.wait_ge(silu_done, sw.gb + g + 1)
                up = PS[:, 2:4, 0:N]
                eng.tensor_tensor(SIL[:, :, 0:N], SIL[:, :, 0:N], up, MUL).then_inc(hm_done, 1)

            def low_h(g):
                eng.wait_ge(hh_done, sw.gb + g + 1)
                eng.tensor_tensor(HAL[:, :, 0:N], SIL[:, :, 0:N], HAH[:, :, 0:N].bitcast(fp32), SUB).then_inc(hl_done, 1)

            def take_down(g):
                for dc in range(DC):
                    eng.wait_ge(dpart, DC * (sw.gb + g) + dc + 1)
                    eng.tensor_tensor(ACC[:, dc, 0:N], ACC[:, dc, 0:N], PS[:, 4 + dc % 4, 0:N], ADD).then_inc(dtaken, 1)

            def body(g, first):
                for j in range(4):
                    rest_unit(eng, *sw.unit(g, j))
                if not first and not small:
                    take_down(g - 2)
                eng.wait_ge(unit_used, used_at(sw.unit0(3) if first else sw.unit(g - 1, 3)))
                product(g - 1)
                for j in range(4, 6):
                    rest_unit(eng, *sw.unit(g, j))
                low_h(g - 1)

            for j in range(sw.ahead, 4):
                rest_unit(eng, *sw.unit0(j))
            body(1, True)
            with eng.Fori(2, sw.G) as g:
                body(g, False)
            if not small:
                take_down(sw.G - 2)
            next_select(sw)
            eng.wait_ge(unit_used, used_at(sw.unit(sw.G - 1, 3)))
            product(sw.G - 1)
            for j in range(2):
                rest_unit(eng, *sw.last(j))
            low_h(sw.G - 1)
            next_block(sw)
            if small:
                eng.wait_ge(unit_used, used_at(sw.last(1)))
                for b in range(4):
                    ins = eng.tensor_copy(ACC[:, 2 * b:2 * b + 2, 0:N],
                                          PS[:, 4 + b, :].rearrange("p (a n) -> p a n", a=2)[:, :, 0:N])
                ins.then_inc(dtaken, DC * sw.G)
            else:
                take_down(sw.G - 1)
            if small:
                eng.sem_inc(dve_acc, 1)
            eng.wait_ge(dtaken, DC * (sw.gb + sw.G + 1))
            eng.sem_inc(acc_done, 1)

        dve_acc, ht_done = sem("acc_cleared"), sem("h_transposed")

        def narrow_pe(eng, sw):
            def gate_up(g, units, w, first):
                for half in range(2):
                    c, d = units(2 * w + half)
                    if half == 0 and not first:
                        eng.wait_ge(hm_done if w else silu_done, sw.gb + g)
                    eng.wait_ge(split, used_at((c, d)))
                    s = c % RING
                    for kk in range(4):
                        k = 4 * half + kk
                        for j, (xt, wt) in enumerate(((HTH, WH), (HTH, WL), (HTL, WH))):
                            ins = eng.matmul(PS[:, 2 * w, 0:256], xt[:, k, 0:P], wt[s][:, kk * 256:(kk + 1) * 256],
                                             start=(k == 0 and j == 0), stop=(k == DC - 1 and j == 2))
                    ins.then_inc(unit_used, 1)

            def turn(g):
                eng.wait_ge(hm_done, sw.gb + g + 1)
                for fc in range(2):
                    ins = eng.transpose(PS[:, 1, fc * P:(fc + 1) * P], SIL[:, 0, fc * P:(fc + 1) * P], ident)
                ins.then_inc(ht_done, 1)

            def down(g, units):
                eng.wait_ge(hl_done, sw.gb + g + 1)
                for fc in range(2):
                    c, d = units(4 + fc)
                    eng.wait_ge(split, used_at((c, d)))
                    for ht, wt in ((HAH, WH), (HAH, WL), (HAL, WH)):
                        for h in range(2):
                            ins = eng.matmul(PS[:, 4 + h, :], ht[:, fc, 0:P], wt[c % RING][:, h * 512:(h + 1) * 512],
                                             start=False, stop=False, skip_group_check=True)
                    ins.then_inc(unit_used, 1)

            for b in range(2):
                ins = eng.matmul(PS[:, 4 + b, :], ZERO[:, 0:P], ZERO[:, :], start=True, stop=False,
                                 skip_group_check=True)
            ins.then_inc(dpart, DC * sw.G)
            for w in range(2):
                gate_up(0, sw.unit0, w, True)
            with eng.Fori(1, sw.G) as g:
                gate_up(g, lambda j: sw.unit(g, j), 0, False)
                turn(g - 1)
                gate_up(g, lambda j: sw.unit(g, j), 1, False)
                down(g - 1, lambda j: sw.unit(g, j))
            block_gather(eng, sw.e + 1, 0, 6)
            turn(sw.G - 1)
            block_turn(eng, sw.e + 1, 0, 6)
            down(sw.G - 1, lambda j: sw.last(j - 4))
            eng.sem_inc(y_t, 4)

        def narrow_act(eng, sw):
            def silu(g, gate):
                eng.wait_ge(unit_used, gate)
                eng.activation(SIL[:, 0, 0:256], PS[:, 0, 0:256], ACT.Silu).then_inc(silu_done, 1)

            def rounded_h(g):
                eng.wait_ge(ht_done, sw.e * sw.G + g + 1)
                eng.activation(HAH[:, :, 0:P], PS[:, 1, 0:256].rearrange("p (f n) -> p f n", n=P), ACT.Copy).then_inc(hh_done, 1)

            def body(g, first):
                for j in range(2):
                    round_unit(eng, *sw.unit(g, j))
                if not first:
                    eng.wait_ge(hl_done, sw.gb + g - 1)
                silu(g - 1, used_at(sw.unit0(1) if first else sw.unit(g - 1, 1)))
                for j in range(2, 4):
                    round_unit(eng, *sw.unit(g, j))
                if not first:
                    eng.wait_ge(unit_used, used_at(sw.unit(g - 1, 5)))
                rounded_h(g - 1)
                for j in range(4, 6):
                    round_unit(eng, *sw.unit(g, j))

            for j in range(sw.ahead, 4):
                round_unit(eng, *sw.unit0(j))
            body(1, True)
            with eng.Fori(2, sw.G) as g:
                body(g, False)
            eng.wait_ge(hl_done, sw.gb + sw.G - 1)
            silu(sw.G - 1, used_at(sw.unit(sw.G - 1, 1)))
            block_rows(eng, sw.e + 1, 0, 6, 0)
            eng.wait_ge(unit_used, used_at(sw.unit(sw.G - 1, 5)))
            rounded_h(sw.G - 1)
            for j in range(2):
                round_unit(eng, *sw.last(j))
            block_scale(eng, sw.e + 1, 0, 6)

        def narrow_dve(eng, sw):
            def product(g, up):
                eng.wait_ge(silu_done, sw.gb + g + 1)
                eng.wait_ge(unit_used, up)
                eng.tensor_tensor(SIL[:, 0, 0:256], SIL[:, 0, 0:256], PS[:, 2, 0:256], MUL).then_inc(hm_done, 1)

            def low_h(g):
                eng.wait_ge(hh_done, sw.gb + g + 1)
                eng.tensor_tensor(HAL[:, :, 0:P], PS[:, 1, 0:256].rearrange("p (f n) -> p f n", n=P),
                                  HAH[:, :, 0:P].bitcast(fp32), SUB).then_inc(hl_done, 1)

            def body(g, first):
                for j in range(2):
                    rest_unit(eng, *sw.unit(g, j))
                product(g - 1, used_at(sw.unit0(3) if first else sw.unit(g - 1, 3)))
                for j in range(2, 4):
                    rest_unit(eng, *sw.unit(g, j))
                low_h(g - 1)
                for j in range(4, 6):
                    rest_unit(eng, *sw.unit(g, j))

            for j in range(sw.ahead, 4):
                rest_unit(eng, *sw.unit0(j))
            body(1, True)
            with eng.Fori(2, sw.G) as g:
                body(g, False)
            block_select(eng, sw.e + 1, 0)
            product(sw.G - 1, used_at(sw.unit(sw.G - 1, 3)))
            block_rows(eng, sw.e + 1, 0, 6, 1)
            low_h(sw.G - 1)
            for j in range(2):
                rest_unit(eng, *sw.last(j))
            block_split(eng, sw.e + 1, 0)
            eng.sem_inc(dve_acc, 1)
            eng.sem_inc(dtaken, DC * sw.G)
            eng.sem_inc(acc_done, 1)

        def swi_load(eng, kind, sw):
            up, dn = up_w[kind], dn_w[kind]
            e = sw.e

            def gu(units, g):
                for w in range(2):
                    for half in range(2):
                        load(eng, *units(2 * w + half), up[w][:, ds(e * DC + 4 * half, 4), ds(g * 256, 256)], 4, 256)

            def dn_(units, g):
                for fc in range(2):
                    load(eng, *units(4 + fc), dn[:, ds(e * 2 * sw.G + 2 * g + fc, 1), :], 1, D)

            gu(sw.unit0, 0)
            with eng.Fori(1, sw.G) as g:
                gu(lambda j: sw.unit(g, j), g)
                dn_(lambda j: sw.unit(g, j), g - 1)
            dn_(lambda j: sw.last(j - 4), sw.G - 1)

        def by_width(eng, count, body, widths=WIDTHS):
            if len(widths) == 1:
                body(widths[0])
                return
            with eng.If(count <= widths[0]):
                body(widths[0])
            with eng.Else():
                by_width(eng, count, body, widths[1:])

        routed = sem("routed")
        AHEAD = 2

        def units_ahead(eng, e, part):
            with eng.If(e < NE - 1):
                for j in range(AHEAD):
                    part(eng, SWI_BASE[1] + j, EXP_G * (e + 1))

        def expert(eng, engine_body):
            with eng.Fori(0, NE) as e:
                count = eng.value_load(CNT[0:1, ds(e, 1)], min_val=0, max_val=T)
                sw = Swi(SWI_BASE[1], EXP_G, FFN_G, 1, e, AHEAD)
                by_width(eng, count, lambda N: engine_body(sw, e, N))

        block = ctx.enter_context(nc.Block())

        @block.sync
        def _(sp):
            sp.dma_start(VROW[0:8, :], a["c"].rearrange("b (k p) -> (b k) p", p=P)).then_inc(loads, 16)
            sp.dma_start(VROW[8:12, :], a["q_norm_g"].rearrange("l (k p) -> (l k) p", p=P)).then_inc(loads, 16)
            sp.dma_start(VROW[12:16, :], a["kv_norm_g"].rearrange("l (k p) -> (l k) p", p=P)).then_inc(loads, 16)
            sp.dma_start(VROW[16:32, :], a["head_norm_g"].rearrange("l (k p) -> (l k) p", p=P)).then_inc(loads, 16)
            sp.dma_start(CST[:, :], a["consts"]).then_inc(loads, 16)
            for j, name in enumerate(("ln1_g", "ln1_b", "ln2_g", "ln2_b")):
                sp.dma_start(NROW[16 * j:16 * j + 16, :], a[name].rearrange("l (k p) -> (l k) p", p=P)).then_inc(loads, 16)
            for m in range(2 * DC):
                mod_load_first(sp, m)
            sp.dma_start(X[:, :, :], x_d).then_inc(x_load, 16)
            for l in range(NL):
                sp.dma_start(BF[:, l, :], a["b_fgate"][l:l + 1, :].to_broadcast([P, HEADS])).then_inc(x_load, 16)
            sp.dma_start(RW[:, :, :], a["router_w"][0].rearrange("(k p) e -> p k e", p=P)).then_inc(x_load, 16)
            for s in range(RING):
                m = max(m for m in range(2 * DC) if m % RING == s)
                sp.wait_ge(modw_used, m + 1)
                load(sp, s, 0, w_in[0, :, 2 * (s % 4):2 * (s % 4) + 2, 512 * (s // 4):512 * (s // 4) + 512], 2, 512)
            for l in range(NL):
                b = BASE[l]
                for c in range(5):
                    n = win_cols(c)
                    for u in range(4):
                        if b + 4 * c + u < RING:
                            continue
                        load(sp, b + 4 * c + u, 0, w_in[l, :, 2 * u:2 * u + 2, 512 * c:512 * c + n], 2, n)
                for j, (w, o) in enumerate(((w_uq, 0), (w_uq, 480), (w_ukv, 0), (w_ukv, 512))):
                    load(sp, b + 20 + j, 0, w[l, :, :, o:o + UP_COLS[j]], 2, UP_COLS[j])
                for half in range(2):
                    for u in range(4):
                        if l == 0 and half == 1 and u == 2:
                            sp.wait_ge(zero_done, 1)
                            for q in range(4):
                                rows = ybuf.rearrange("(q p r) d -> q p (r d)", q=4, p=P)[q].rearrange("p (r d) -> p r d", d=512)
                                sp.dma_start(rows, ZERO[:, :].bitcast(fp32).unsqueeze(1).to_broadcast([P, 16, 512])
                                             ).then_inc(y_st, 16)
                        load(sp, b + 24 + 4 * half + u, 0, w_o[l, :, O_CHUNKS[u], half * 512:(half + 1) * 512], 2, 512)
                if l == 0:
                    swi_load(sp, 0, Swi(SWI_BASE[0], FFN_G, 0, 0))
                else:
                    with sp.Fori(0, NE) as e:
                        swi_load(sp, 1, Swi(SWI_BASE[1], EXP_G, FFN_G, 1, e))
            for i in range(TC):
                sp.wait_ge(ln_x, 12 + i + 1)
                sp.dma_start(out_d[:, i, :], X[:, i, :]).then_inc(sem("out_stored"), 16)
            sp.wait_ge(sem("out_stored"), 16 * TC)

        @block.gpsimd
        def _(pool):
            step = [0]

            def link(ins):
                step[0] += 1
                ins.then_inc(pool_step, 1)
                pool.wait_ge(pool_step, step[0])

            mod_load(pool, 0)
            mod_load(pool, 1)
            for l in range(NL):
                if l:
                    pool.wait_ge(ln_n, 8)
                pool.memset(QA[:, :, :, HD + 1:HD + 2], 1.0)
                pool.memset(KA[:, :, :, HD:HD + 1], 1.0).then_inc(sem("columns_set"), 1)
                for c in range(5):
                    for q in MOD_WHEN[l, c]:
                        mod_load(pool, q)
                pool.wait_ge(z_out, 20 * l + 16)
                pool.wait_ge(mod_red, 6 if l == 0 else 12)
                pool.dma_start(WCV[:, :, :], a["w_conv"][l:l + 1, :, :].rearrange("l k c -> l (k c)").to_broadcast([P, 768])
                               .rearrange("p (k c) -> p k c", k=3)).then_inc(wcv_load, 16)
                ZCc, Zh, Zb = ZR[:, :, ZC:ZC + 256], ZR[:, :, ZH:ZH + 256], ZR[:, :, ZB:ZB + 256]
                pool.memset(U1[0:1, 0, :], 0.0)
                pool.memset(U2[0:2, 0, :], 0.0)
                link(pool.tensor_tensor(ZCc, ZCc, Zh, MUL))
                for s, U in ((1, U1), (2, U2)):
                    pool.dma_start(U[s:112 + s, :, :], ZR[0:112, :, ZC:ZC + 256]).then_inc(shifted, 16)
                    pool.dma_start(U[112 + s:P, :, :], ZR[112:P - s, :, ZC:ZC + 256]).then_inc(shifted, 16)
                    pool.dma_start(U[0:s, 1:TC, :], ZR[P - s:P, 0:TC - 1, ZC:ZC + 256]).then_inc(shifted, 16)
                oc = OA[:, :, 12:16, :].rearrange("p i h d -> p i (h d)")

                def tap(k):
                    return WCV[:, k:k + 1, :].to_broadcast([P, TC, 256])
                pool.wait_ge(wcv_load, 16 * (l + 1))
                link(pool.tensor_tensor(Zh, ZCc, tap(2), MUL))
                pool.wait_ge(shifted, 96 * (l + 1))
                pool.tensor_tensor(U1[:, :, :], U1[:, :, :], tap(1), MUL)
                link(pool.tensor_tensor(U2[:, :, :], U2[:, :, :], tap(0), MUL))
                link(pool.tensor_tensor(Zh, Zh, U1[:, :, :], ADD))
                link(pool.tensor_tensor(Zh, Zh, U2[:, :, :], ADD))
                pool.tensor_tensor(oc, Zh, Zb, MUL).then_inc(conv_done, 1)
                pool.wait_ge(conv_done, l + 1)
                att_pool(pool, l, 0)
                att_pool(pool, l, 1)
                ln_rows(pool, 2 * l)
                affine(pool, 2 * l, TE["h2", l] + 8)
                if l == 0:
                    pool.wait_ge(te_t, TE["o", 0] + 8)
                    for q in (6, 7):
                        mod_load(pool, q, lambda k: mod_sum_pool(pool, q, k))
                    ln_rows(pool, 1)
            ln_rows(pool, 3)
            pool.wait_ge(routed, 2)
            pool.wait_ge(y_t, 4 * NE)
            pool.wait_ge(te_l, TE_X + 8 * NE + 2)
            for i in range(TC):
                for j in range(2):
                    pool.indirect_dma_start(
                        out=YG[i][j][:, :], out_offset=None, in_=ybuf[:, :],
                        in_offset=bass.IndirectOffsetOnAxis(ap=ROWI[:, j, i:i + 1], axis=0)).then_inc(sem(f"y_back{i}"), 16)
            affine(pool, 3)

        @block.scalar
        def _(act):
            act.wait_ge(vrow_t, 1)
            act.activation(CACT[:, :], PS[:, 0, 0:DC], ACT.Silu).then_inc(y_out, 4)
            act.copy(VCOL[:, :], PS[:, 0, DC:32]).then_inc(vcol, 1)
            act.wait_ge(vrow_t, 2)
            act.copy(NCOL[:, :], PS[:, 1, 0:64]).then_inc(vcol, 1)
            act.wait_ge(x_load, 16 * 4)
            act.copy(RWH[:, :, :], RW[:, :, :]).then_inc(sem("router_rounded"), 1)
            for l in range(NL):
                b = BASE[l]
                if l:
                    for n in range(4):
                        round_unit(act, b + n, 0)
                    ln_act(act, 1)
                if l:
                    act.wait_ge(ncol, 6)
                else:
                    act.wait_ge(mod_out, 2)
                for k in range(DC):
                    te_scale(act, TE["h1", l] + k, 0, k, T, *((NMC[:, 1, j, k:k + 1] for j in range(2)) if l else
                                                          (scale_col(0, 0, k), shift_col(0, 0, k))))

                def z_take(c):
                    for i in range(TC):
                        bank = c % 2 * 4 + i
                        act.wait_ge(unit_used, b + 4 * c + 4)
                        src = PS[:, bank, :]

                        def heads(s, lo, hi):
                            return s[:, lo:hi].rearrange("p (h d) -> p h d", d=HD)
                        if c == 0:
                            act.activation(QA[:, :, i, 0:HD], heads(src, 0, 384), ACT.Copy, scale=HD ** -0.5)
                            ins = act.copy(KA[:, 0:2, i, 0:HD], heads(src, 384, 512))
                        elif c == 1:
                            act.copy(KA[:, 2:6, i, 0:HD], heads(src, 0, 256))
                            ins = act.copy(VA[:, 0:4, i, :], heads(src, 256, 512))
                        elif c == 2:
                            if i == 0 and l:
                                act.wait_ge(ln_x, 8)
                            act.copy(VA[:, 4:6, i, :], heads(src, 0, 128))
                            ins = act.copy(ZR[:, i, 0:384], src[:, 128:512])
                        else:
                            n = win_cols(c)
                            ins = act.copy(ZR[:, i, 384 + 512 * (c - 3):384 + 512 * (c - 3) + n], src[:, 0:n])
                        ins.then_inc(z_out, 1)
                for c in range(5):
                    for u in range(4):
                        if l == 0 or c:
                            round_unit(act, b + 4 * c + u, 0, 2 * win_cols(c))
                    if c:
                        z_take(c - 1)
                    if c == 4:
                        act.wait_ge(gate_n, l + 1)
                        act.activation(FG[:, 2, :], FG[:, 1, :], ACT.Exp).then_inc(gate_l, 1)
                        act.wait_ge(gate_l, 2 * l + 1)
                        act.activation(FG[:, 2, :], FG[:, 2, :], ACT.Ln, bias=1.0).then_inc(gate_l, 1)
                z_take(4)
                act.wait_ge(z_out, 20 * (l + 1))
                for i in range(TC):
                    for w in range(2):
                        ins = act.activation(CN[:, i, w * 256:(w + 1) * 256], ZR[:, i, ZQ + w * 256:ZQ + (w + 1) * 256],
                                             ACT.Square, accum_out=SS[:, 0, 2 * i + w:2 * i + w + 1])
                ins.then_inc(ssq, 1)
                act.wait_ge(ssq, l + 1)
                act.activation(SS[:, 0, 0:8], SS[:, 0, 0:8], ACT.Sqrt, bias=CST[:, C_EPS + 1:C_EPS + 2],
                               scale=1.0 / 256).then_inc(rstd_s, 1)
                for k in range(4):
                    g = VCOL[:, (0, 4)[k // 2] + 2 * l + k % 2:(0, 4)[k // 2] + 2 * l + k % 2 + 1]
                    te_scale(act, TE["c", l] + k, 0, 4 + k, T, g)
                for j in range(4):
                    round_unit(act, b + 20 + j, 0, 2 * UP_COLS[j])
                att_act(act, l, 0)
                for j in range(4):
                    for i in range(TC):
                        act.wait_ge(unit_used, b + 20 + j + 1)
                        src = PS[:, j % 2 * 4 + i, :]
                        if j == 0:
                            act.wait_ge(A["staged"], ATT(l, 1))
                            ins = act.activation(QA[:, 0:5, i, :], src[:, 0:480].rearrange("p (h d) -> p h d", d=96),
                                                 ACT.Copy, scale=KQ_MLA ** -0.5)
                        elif j == 1:
                            ins = act.activation(QA[:, 5, i, :], src[:, 0:96], ACT.Copy, scale=KQ_MLA ** -0.5)
                        else:
                            h0, h1 = (0, 4) if j == 2 else (4, 6)
                            s = src[:, 0:P * (h1 - h0)].rearrange("p (h d) -> p h d", d=P)
                            act.copy(KA[:, h0:h1, i, 0:HD], s[:, :, 0:HD])
                            ins = act.copy(VA[:, h0:h1, i, :], s[:, :, HD:P])
                        ins.then_inc(up_out, 1)
                for n in range(24, 30):
                    round_unit(act, b + n, 0)
                att_act(act, l, 1)
                act.wait_ge(A["oev"], ATT(l, 1) + HEADS)
                act.wait_ge(conv_done, l + 1)
                for i in range(TC):
                    act.activation(OSQ[:, i, :], OA[:, i, :, :].rearrange("p h d -> p (h d)"), ACT.Square).then_inc(osq, 1)
                act.wait_ge(on_sum, 4 * (l + 1))
                act.activation(SS[:, 1, :], SS[:, 1, :], ACT.Sqrt, bias=CST[:, C_EPS + 1:C_EPS + 2],
                               scale=1.0 / HD).then_inc(on_sqrt, 1)
                for k in range(DC):
                    g = VCOL[:, 8 + 8 * l + O_ORDER[k]:8 + 8 * l + O_ORDER[k] + 1]
                    te_scale(act, TE["o", l] + k, 0, k, T, g)
                for n in range(30, 32):
                    round_unit(act, b + n, 0)
                ln_act(act, 2 * l)
                act.wait_ge(ncol, 6 * l + 3)
                for k in range(DC):
                    te_scale(act, TE["h2", l] + k, 0, k, T, *(NMC[:, 2 * l, j, k:k + 1] for j in range(2)))
                if l == 0:
                    swi_act(act, Swi(SWI_BASE[0], FFN_G, 0, 0), T)
                else:
                    for j in range(AHEAD):
                        round_unit(act, SWI_BASE[1] + j, 0)
            act.wait_ge(sem("logits_t"), 1)
            act.copy(TMP[0:NE, 0, :], PS[0:NE, 2, :]).then_inc(sem("logits_out"), 1)
            for i in range(TC):
                act.wait_ge(ln_x, 8 + i + 1)
                act.copy(XH[:, i, :], X[:, i, :]).then_inc(sem("x_rounded"), 1)
            act.wait_ge(sem("route_diff"), 1)
            act.activation(RT1[:, 5, :], RT1[:, 4, :], ACT.Exp).then_inc(sem("route_exp"), 1)
            act.wait_ge(routed, 2)
            act.wait_ge(y_st, CLEARED)
            block_rows(act, 0, 0, 6, 0)
            block_scale(act, 0, 0, 6)

            def next_block(sw):
                block_rows(act, sw.e + 1, 0, 0, 0)
                block_scale(act, sw.e + 1, 0, 0)

            def body(sw, e, N):
                blocks = (N + P - 1) // P
                for j in range(1, blocks):
                    block_rows(act, e, j, j % 2 * 2, 0)
                    if j > 1:
                        block_scale(act, e, j - 1, (j - 1) % 2 * 2)
                if blocks > 1:
                    block_scale(act, e, blocks - 1, (blocks - 1) % 2 * 2)
                no_blocks(act, e, blocks, (xg_a, 0, 1), (te_a, TE_X, 2))
                if N == P:
                    narrow_act(act, sw)
                else:
                    swi_act(act, sw, N, next_block)
                units_ahead(act, e, round_unit)
                for sb in range(blocks):
                    if N == P:
                        act.wait_ge(unit_used, used_at(sw.last(1)))
                    else:
                        act.wait_ge(y_t, 4 * e + sb + 1)
                    if sb == 0:
                        act.wait_ge(y_st, CLEARED + 16 * e)
                    ins = act.copy(YT[:, sb, 0:512], PS[:, 4 + sb % 2 * 2, :])
                    ins.then_inc(y_out, 1 if sb < blocks - 1 else 5 - blocks)
                act.wait_ge(sem("y_out_dve"), 4 * e + 8)
                act.wait_ge(y_out, 4 * e + 8)
                yv = ybuf.rearrange("(b p) d -> p b d", p=P)
                act.dma_start(yv[:, ds(4 * e, blocks), :], YT[:, 0:blocks, :]).then_inc(y_st, 16)
            expert(act, body)

            def weigh(i):
                act.wait_ge(sem(f"y_back{i}"), 32)
                act.activation(YG[i][0][:, :], YG[i][0][:, :], ACT.Copy, scale=RT1[:, 6, i:i + 1]).then_inc(sem("y_weighed"), 1)
            weigh(0)
            weigh(1)
            ln_act(act, 3, lambda i: weigh(i + 2) if i + 2 < TC else None)
            act.wait_ge(y_st, CLEARED + 16 * NE)

        @block.vector
        def _(dv):
            def link(ins):
                steps["dve"] += 1
                ins.then_inc(dve, 1)
                dv.wait_ge(dve, steps["dve"])

            dv.memset(ZERO[:, :].bitcast(fp32), 0.0).then_inc(zero_done, 1)
            dv.sem_inc(dtaken, DC)
            dv.wait_ge(vcol, 1)
            mod_sum(dv, 0)
            mod_sum(dv, 1)
            mod_take(dv, 0, 4)
            mod_take(dv, 1, 6)
            dv.wait_ge(sem("router_rounded"), 1)
            dv.tensor_tensor(RWL[:, :, :], RW[:, :, :], RWH[:, :, :].bitcast(fp32), SUB).then_inc(sem("router_split"), 1)
            for l in range(NL):
                b = BASE[l]
                if l:
                    for n in range(4):
                        rest_unit(dv, b + n, 0)
                    mod_take(dv, 6, 2)
                    mod_take(dv, 7, 3)
                    norm_cols(dv, 1)
                    ln_dve(dv, 1, lambda i: PS[:, 2 * i:2 * i + 2, :], lambda i: dv.wait_ge(sem("ffn_t"), i + 1))
                for k in range(DC):
                    te_split(dv, TE["h1", l] + k, 0, k, T)
                if l:
                    affine(dv, 1, TE["h1", 1] + 8)
                for c in range(5):
                    for u in range(4):
                        if l == 0 or c:
                            rest_unit(dv, b + 4 * c + u, 0, 2 * win_cols(c))
                    for q in MOD_WHEN[l, c]:
                        mod_sum(dv, q)
                    for j, q in enumerate(MOD_WHEN[l, c]):
                        mod_take(dv, q, mod_bank(c, j))
                    if c == 4:
                        dv.wait_ge(z_out, 20 * l + 12)
                        fg = [FG[:, j, :].rearrange("p (i h) -> p i h", h=HEADS) for j in range(4)]
                        link(dv.tensor_tensor(fg[0], ZR[:, :, ZF:ZF + HEADS], BF[:, l:l + 1, :].to_broadcast([P, TC, HEADS]), ADD))
                        link(dv.tensor_scalar(FG[:, 1, :], FG[:, 0, :], -1.0, None, MUL))
                        dv.tensor_tensor(FG[:, 1, :], FG[:, 0, :], FG[:, 1, :], MIN).then_inc(gate_n, 1)
                        dv.wait_ge(gate_l, 2 * (l + 1))
                        dv.scalar_tensor_tensor(out=FG[:, 3, :], in0=FG[:, 0, :], scalar=0.0, in1=FG[:, 2, :],
                                                op0=MIN, op1=SUB).then_inc(gate_f, 1)
                dv.wait_ge(gate_s, l + 1)
                f = PS[:, 4, 0:TC * HEADS].rearrange("p (i h) -> p h i", h=HEADS)
                dv.tensor_scalar(QA[:, :, :, HD], f, 1.0, None, MUL).then_inc(gate_q, 1)
                dv.tensor_scalar(KA[:, :, :, HD + 1], f, -1.0, None, MUL).then_inc(gate_q, 1)
                dv.wait_ge(z_out, 20 * (l + 1))
                cos, sin = (CST[:, o:o + 64].rearrange("p (i d) -> p i d", d=16) for o in (C_COS, C_SIN))
                x1, x2 = ZR[:, :, ZR_:ZR_ + 16], ZR[:, :, ZR_ + 16:ZR_ + 32]
                kt = [RTK[:, j, :].rearrange("p (i d) -> p i d", d=16) for j in range(4)]
                dv.tensor_tensor(kt[0], x1, cos, MUL)
                dv.tensor_tensor(kt[1], x2, sin, MUL)
                dv.tensor_tensor(kt[2], x2, cos, MUL)
                link(dv.tensor_tensor(kt[3], x1, sin, MUL))
                dv.tensor_tensor(KRO[:, :, 0:16], kt[0], kt[1], SUB)
                dv.tensor_tensor(KRO[:, :, 16:32], kt[2], kt[3], ADD).then_inc(kr_done, 1)
                dv.wait_ge(rstd_s, l + 1)
                link(dv.reciprocal(SS[:, 0, 0:8], SS[:, 0, 0:8]))
                cn = CN[:, :, :].rearrange("p i (w c) -> p i w c", w=2)
                dv.tensor_tensor(cn, ZR[:, :, ZQ:ZQ + 512].rearrange("p i (w c) -> p i w c", w=2),
                                 SS[:, 0, 0:8].rearrange("p (i w) -> p i w", w=2).unsqueeze(3).to_broadcast([P, TC, 2, 256]),
                                 MUL).then_inc(kr_done, 1)
                for k in range(4):
                    te_split(dv, TE["c", l] + k, 0, k, T)
                for j in range(4):
                    rest_unit(dv, b + 20 + j, 0, 2 * UP_COLS[j])
                att_dve(dv, l, 0)
                dv.wait_ge(up_out, 16 * l + 8)
                q1, q2 = QA[:, :, :, 64:80], QA[:, :, :, 80:96]
                cb, sb_ = (z.unsqueeze(1).to_broadcast([P, HEADS, TC, 16]) for z in (cos, sin))
                rt = [RTMP[:, j, :].rearrange("p (h i d) -> p h i d", h=HEADS, d=16) for j in range(4)]
                dv.tensor_tensor(rt[0], q1, cb, MUL)
                dv.tensor_tensor(rt[1], q2, sb_, MUL)
                dv.tensor_tensor(rt[2], q2, cb, MUL)
                link(dv.tensor_tensor(rt[3], q1, sb_, MUL))
                dv.tensor_tensor(q1, rt[0], rt[1], SUB).then_inc(rope_done, 1)
                dv.tensor_tensor(q2, rt[2], rt[3], ADD).then_inc(rope_done, 1)
                dv.wait_ge(A["staged"], ATT(l, 1))
                dv.tensor_copy(KA[:, :, :, 64:96], KRO[:, :, :].unsqueeze(1).to_broadcast([P, HEADS, TC, ROPE])).then_inc(rope_done, 1)
                for n in range(24, 30):
                    rest_unit(dv, b + n, 0)
                att_dve(dv, l, 1)
                for i in range(TC):
                    dv.wait_ge(osq, 4 * l + i + 1)
                    dv.tensor_reduce(SS[:, 1, 16 * i:16 * i + 16], OSQ[:, i, :].rearrange("p (h d) -> p h d", d=HD),
                                     AX.X, ADD).then_inc(on_sum, 1)
                dv.wait_ge(on_sqrt, l + 1)
                dv.reciprocal(SS[:, 1, :], SS[:, 1, :]).then_inc(on_rd, 1)
                dv.wait_ge(on_rd, l + 1)
                for i in range(TC):
                    dv.tensor_tensor(OA[:, i, :, :], OA[:, i, :, :],
                                     SS[:, 1, 16 * i:16 * i + 16].unsqueeze(2).to_broadcast([P, 16, HD]), MUL).then_inc(on_done, 1)
                for k in range(DC):
                    te_split(dv, TE["o", l] + k, 0, k, T)
                for n in range(30, 32):
                    rest_unit(dv, b + n, 0)
                norm_cols(dv, 2 * l)
                ln_dve(dv, 2 * l, lambda i: PS[:, i::4, :], lambda i: dv.wait_ge(unit_used, b + PER_LAYER))
                for k in range(DC):
                    te_split(dv, TE["h2", l] + k, 0, k, T)
                if l == 0:
                    clear_acc(dv, Swi(SWI_BASE[0], FFN_G, 0, 0), T)
                    swi_dve(dv, Swi(SWI_BASE[0], FFN_G, 0, 0), T)
                else:
                    for j in range(AHEAD):
                        rest_unit(dv, SWI_BASE[1] + j, 0)
            v8 = [RT8[:, j, :].rearrange("p (i e) -> p i e", e=NE) for j in range(10)]
            v1 = [RT1[:, j, :] for j in range(8)]

            def b1(j):
                return RT1[:, j, :].unsqueeze(2).to_broadcast([P, TC, NE])
            rev = CST[:, C_REV:C_REV + NE].unsqueeze(1).to_broadcast([P, TC, NE])
            row0 = CST[:, C_ROW:C_ROW + NE].unsqueeze(1).to_broadcast([P, TC, NE])
            dv.wait_ge(sem("logits"), 1)
            link(dv.tensor_copy(RT8[:, 0, :], PS[:, 0, 0:TC * NE]))
            for c in range(2):
                link(dv.tensor_reduce(v1[c], v8[0], AX.X, MAX))
                link(dv.tensor_tensor(v8[1], v8[0], b1(c), ALU.is_equal))
                link(dv.tensor_tensor(v8[1], v8[1], rev, MUL))
                link(dv.tensor_reduce(v1[2], v8[1], AX.X, MAX))
                link(dv.tensor_tensor(v8[3 + c], b1(2), rev, ALU.is_equal))
                if c == 0:
                    link(dv.scalar_tensor_tensor(out=RT8[:, 0, :], in0=RT8[:, 3, :], scalar=-3.0 * BIG, in1=RT8[:, 0, :],
                                                 op0=MUL, op1=ADD))
            dv.tensor_tensor(v1[4], v1[1], v1[0], SUB).then_inc(sem("route_diff"), 1)
            dv.tensor_tensor(RT8[:, 5, :], RT8[:, 3, :], RT8[:, 4, :], ADD).then_inc(sem("chosen"), 1)
            dv.wait_ge(sem("places"), 1)
            dv.tensor_copy(CNT[:, :], PS[:, 1, 32:40]).then_inc(routed, 1)
            link(dv.tensor_copy(RT8[:, 6, :], PS[:, 1, 0:32]))
            link(dv.scalar_tensor_tensor(out=RT8[:, 7, :], in0=RT8[:, 6, :], scalar=1.0, in1=RT8[:, 5, :], op0=ADD, op1=MUL))
            dv.memset(PLACE[:, :, NE:NE + 1], -1.0)
            link(dv.tensor_scalar(PLACE[:, :, 0:NE], v8[7], -1.0, None, ADD))
            link(dv.tensor_tensor(v8[6], v8[6], row0, ADD))
            for c in range(2):
                link(dv.tensor_tensor(RT8[:, 8, :], RT8[:, 6, :], RT8[:, 3 + c, :], MUL))
                link(dv.tensor_reduce(v1[2], v8[8], AX.X, ADD))
                link(dv.tensor_copy(ROWI[:, c, :], v1[2]))
            for i in range(TC):
                dv.wait_ge(sem("x_rounded"), i + 1)
                ins = dv.tensor_tensor(XL[:, i, :], X[:, i, :], XH[:, i, :].bitcast(fp32), SUB)
            link(ins)
            dv.sem_inc(routed, 1)
            block_select(dv, 0, 0, True)
            dv.wait_ge(sem("route_exp"), 1)
            link(dv.tensor_scalar(v1[6], v1[5], 1.0, None, ADD))
            link(dv.reciprocal(v1[6], v1[6]))
            link(dv.tensor_tensor(v1[7], v1[5], v1[6], MUL))
            block_rows(dv, 0, 0, 6, 1)
            block_split(dv, 0, 0)

            def next_block(sw):
                block_rows(dv, sw.e + 1, 0, 0, 1)
                block_split(dv, sw.e + 1, 0)

            def body(sw, e, N):
                blocks = (N + P - 1) // P
                for j in range(1, min(3, blocks)):
                    block_select(dv, e, j)
                if N > 256:
                    clear_acc(dv, sw, N)
                for j in range(1, blocks):
                    if j > 1 and j + 1 < blocks:
                        block_select(dv, e, j + 1)
                    block_rows(dv, e, j, j % 2 * 2, 1)
                    if j > 1:
                        block_split(dv, e, j - 1)
                if blocks > 1:
                    block_split(dv, e, blocks - 1)
                no_blocks(dv, e, blocks, (sel_done, 0, 1), (xg_v, 0, 1), (te_h, TE_X, 2), (te_l, TE_X, 2))
                if N == P:
                    narrow_dve(dv, sw)
                else:
                    swi_dve(dv, sw, N, lambda sw: block_select(dv, sw.e + 1, 0), next_block)
                units_ahead(dv, e, rest_unit)
                for sb in range(blocks):
                    if N == P:
                        dv.wait_ge(unit_used, used_at(sw.last(1)))
                    else:
                        dv.wait_ge(y_t, 4 * e + sb + 1)
                    if sb == 0:
                        dv.wait_ge(y_st, CLEARED + 16 * e)
                    ins = dv.tensor_copy(YT[:, sb, 512:1024], PS[:, 5 + sb % 2 * 2, :])
                    ins.then_inc(sem("y_out_dve"), 1 if sb < blocks - 1 else 5 - blocks)
            dv.memset(ACC[:, :, :], 0.0).then_inc(sem("y_out_dve"), 4)
            dv.wait_ge(sem("y_out_dve"), 4)
            expert(dv, body)
            link(dv.tensor_tensor(X[:, :, :], XH[:, :, :].bitcast(fp32), XL[:, :, :].bitcast(fp32), ADD))

            def ready(i):
                dv.wait_ge(sem("y_weighed"), i + 1)
                y0, y1 = YG[i]
                link(dv.scalar_tensor_tensor(out=y0[:, :], in0=y1[:, :], scalar=RT1[:, 7, i:i + 1], in1=y0[:, :],
                                             op0=MUL, op1=ADD))
            ln_dve(dv, 3, lambda i: YG[i][0][:, :].rearrange("p (a b) -> p a b", a=2), ready)

        @block.tensor
        def _(pe):
            pe.wait_ge(loads, 16 * 9)
            pe.transpose(PS[:, 0, 0:32], VROW[:, :], CST[0:32, C_ID:C_ID + 32]).then_inc(vrow_t, 1)
            pe.transpose(PS[:, 1, 0:64], NROW[:, :], CST[0:64, C_ID:C_ID + 64]).then_inc(vrow_t, 1)
            mod_reduce(pe, 0, 4)
            mod_reduce(pe, 1, 6)
            pe.wait_ge(mod_out, 2)
            pe.wait_ge(x_load, 16 * 4)
            pe.wait_ge(vcol, 2)
            for l in range(NL):
                b = BASE[l]
                if l:
                    pe.wait_ge(hm_done, FFN_G)
                    mod_reduce(pe, 6, 2)
                    mod_reduce(pe, 7, 3)
                    pe.wait_ge(acc_done, 1)
                    for i in range(TC):
                        if i == 1:
                            pe.wait_ge(mod_out, 8)
                        for k in range(DC):
                            ins = pe.transpose(PS[:, 2 * i + k // 4, k % 4 * P:(k % 4 + 1) * P],
                                               ACC[:, k, i * P:(i + 1) * P], ident)
                        ins.then_inc(sem("ffn_t"), 1)
                    pe.wait_ge(ln_n, 8)
                for k in range(DC):
                    te_transposes(pe, TE["h1", l] + k, k, [X[:, i, k * P:(k + 1) * P] for i in range(TC)])
                pe.wait_ge(te_l, TE["h1", l] + 8)
                for c in range(5):
                    n = win_cols(c)
                    for u in range(4):
                        pe.wait_ge(split, b + 4 * c + u + 1)
                        s = (b + 4 * c + u) % RING
                        for i in range(TC):
                            if u == 0 and c >= 2:
                                pe.wait_ge(z_out, 20 * l + 4 * (c - 2) + i + 1)
                            if u == 0 and i == 2 and c:
                                pe.wait_ge(mod_out, MOD_WHEN[l, c - 1][-1] + 1)
                            for kk in range(2):
                                k = 2 * u + kk
                                for j, (ht, wt) in enumerate(((HTH, WH), (HTH, WL), (HTL, WH))):
                                    ins = pe.matmul(PS[:, c % 2 * 4 + i, 0:n], ht[:, k, i * P:(i + 1) * P],
                                                    wt[s][:, kk * n:(kk + 1) * n],
                                                    start=(k == 0 and j == 0), stop=(k == DC - 1 and j == 2))
                        ins.then_inc(unit_used, 1)
                    for j, q in enumerate(MOD_WHEN[l, c]):
                        if c:
                            pe.wait_ge(z_out, 20 * l + 4 * c)
                        mod_reduce(pe, q, mod_bank(c, j))
                pe.wait_ge(z_out, 20 * l + 16)
                pe.wait_ge(mod_out, 6 if l == 0 else 12)
                pe.wait_ge(gate_f, l + 1)
                for i in range(TC):
                    for j in range(i + 1):
                        w = CST[:, C_TRI:C_TRI + P] if j == i else ones
                        ins = pe.matmul(PS[:, 4, i * HEADS:(i + 1) * HEADS], w, FG[:, 3, j * HEADS:(j + 1) * HEADS],
                                        start=(j == 0), stop=(j == i))
                ins.then_inc(gate_s, 1)
                pe.wait_ge(kr_done, 2 * (l + 1))
                pe.wait_ge(gate_q, 2 * (l + 1))
                pe.wait_ge(z_out, 20 * (l + 1))
                for k in range(4):
                    te_transposes(pe, TE["c", l] + k, 4 + k, [CN[:, i, k * P:(k + 1) * P] for i in range(TC)])
                att_pe(pe, l, 0)
                pe.wait_ge(A["oev"], ATT(l, 1))
                for j in range(4):
                    n = UP_COLS[j]
                    s = (b + 20 + j) % RING
                    pe.wait_ge(split, b + 20 + j + 1)
                    k0 = 0 if j < 2 else 2
                    for i in range(TC):
                        if j >= 2:
                            pe.wait_ge(up_out, 16 * l + 4 * (j - 2) + i + 1)
                        for kk in range(2):
                            for z, (ht, wt) in enumerate(((HTH, WH), (HTH, WL), (HTL, WH))):
                                ins = pe.matmul(PS[:, j % 2 * 4 + i, 0:n], ht[:, k0 + kk, i * P:(i + 1) * P],
                                                wt[s][:, kk * n:(kk + 1) * n],
                                                start=(kk == 0 and z == 0), stop=(kk == 1 and z == 2))
                    ins.then_inc(unit_used, 1)
                att_pe(pe, l, 1)
                pe.wait_ge(A["oev"], ATT(l, 1) + HEADS)
                pe.wait_ge(on_done, 4 * (l + 1))
                for k in range(DC):
                    te_transposes(pe, TE["o", l] + k, k,
                                  [OA[:, i, 2 * k:2 * k + 2, :].rearrange("p h d -> p (h d)") for i in range(TC)])
                pe.wait_ge(te_l, TE["o", l] + 8)
                for half in range(2):
                    for u in range(4):
                        n = b + 24 + 4 * half + u
                        pe.wait_ge(split, n + 1)
                        for i in range(TC):
                            for kk in range(2):
                                k = 2 * u + kk
                                for j, (ht, wt) in enumerate(((HTH, WH), (HTH, WL), (HTL, WH))):
                                    ins = pe.matmul(PS[:, 4 * half + i, :], ht[:, k, i * P:(i + 1) * P],
                                                    wt[n % RING][:, kk * 512:(kk + 1) * 512],
                                                    start=(k == 0 and j == 0), stop=(k == DC - 1 and j == 2))
                        ins.then_inc(unit_used, 1)
                pe.wait_ge(ln_n, 8 * l + 4)
                for k in range(DC):
                    te_transposes(pe, TE["h2", l] + k, k, [X[:, i, k * P:(k + 1) * P] for i in range(TC)])
                pe.wait_ge(te_l, TE["h2", l] + 8)
                if l == 0:
                    swi_pe(pe, Swi(SWI_BASE[0], FFN_G, 0, 0), T)
            pe.wait_ge(sem("router_split"), 1)
            for k in range(DC):
                for j, (ht, wt) in enumerate(((HTH, RWH), (HTH, RWL), (HTL, RWH))):
                    ins = pe.matmul(PS[0:NE, 2, :], wt[:, k, :], ht[:, k, :],
                                    start=(k == 0 and j == 0), stop=(k == DC - 1 and j == 2))
            ins.then_inc(sem("logits_t"), 1)
            pe.wait_ge(sem("logits_out"), 1)
            for i in range(TC):
                ins = pe.transpose(PS[:, 0, i * NE:(i + 1) * NE], TMP[0:NE, 0, i * P:(i + 1) * P], CST[0:NE, C_ID:C_ID + NE])
            ins.then_inc(sem("logits"), 1)
            pe.wait_ge(sem("chosen"), 1)
            for i in range(TC + 1):
                for j in range(min(i + 1, TC)):
                    w = CST[:, C_STRI:C_STRI + P] if j == i else ones
                    ins = pe.matmul(PS[:, 1, i * NE:(i + 1) * NE], w, RT8[:, 5, j * NE:(j + 1) * NE],
                                    start=(j == 0), stop=(j == min(i, TC - 1)))
            ins.then_inc(sem("places"), 1)
            pe.wait_ge(zero_done, 1)
            pe.wait_ge(routed, 2)
            block_gather(pe, 0, 0, 6)
            block_turn(pe, 0, 0, 6)

            def next_block(sw):
                pe.wait_ge(hm_done, sw.gb + sw.G)
                block_gather(pe, sw.e + 1, 0, 0)
                block_turn(pe, sw.e + 1, 0, 0)

            def body(sw, e, N):
                blocks = (N + P - 1) // P
                for j in range(1, blocks):
                    if j > 1:
                        pe.wait_ge(te_a, TE_X + 2 * (4 * e + j - 1))
                    block_gather(pe, e, j, j % 2 * 2)
                    if j > 1:
                        block_turn(pe, e, j - 1, (j - 1) % 2 * 2)
                if blocks > 1:
                    block_turn(pe, e, blocks - 1, (blocks - 1) % 2 * 2)
                no_blocks(pe, e, blocks, (gathered, 0, 1), (te_t, TE_X, 2))
                if N > P:
                    pe.sem_inc(ht_done, EXP_G)
                pe.wait_ge(y_out, 4 * e + 4)
                pe.wait_ge(sem("y_out_dve"), 4 * e + 4)
                pe.wait_ge(te_l, TE_X + 8 * e + 8)
                if N == P:
                    narrow_pe(pe, sw)
                    return
                swi_pe(pe, sw, N, next_block)
                pe.wait_ge(acc_done, e + 2)
                for sb in range(blocks):
                    if sb >= 2:
                        pe.wait_ge(y_out, 4 * e + sb + 3)
                        pe.wait_ge(sem("y_out_dve"), 4 * e + sb + 3)
                    for k in range(DC):
                        ins = pe.transpose(PS[:, 4 + sb % 2 * 2 + k // 4, k % 4 * P:(k % 4 + 1) * P],
                                           ACC[:, k, sb * P:(sb + 1) * P], ident)
                    ins.then_inc(y_t, 1 if sb < blocks - 1 else 5 - blocks)
            expert(pe, body)


_NAMES = ['x', 'c', 'w_mod', 'b_mod', 'w_in', 'b_fgate', 'w_conv', 'q_norm_g', 'kv_norm_g', 'w_uq', 'w_ukv',
          'head_norm_g', 'w_o', 'ln1_g', 'ln1_b', 'ln2_g', 'ln2_b', 'ffn_w_gate', 'ffn_w_up', 'ffn_w_down',
          'router_w', 'exp_w_gate', 'exp_w_up', 'exp_w_down']


def constants():
    import numpy as np
    c = np.zeros((P, C_W), np.float32)
    r = np.arange(P)
    c[:, C_ID:C_ID + P] = np.eye(P)
    c[:, C_ONE:C_ONE + P] = 1
    c[:, C_TRI:C_TRI + P] = r[:, None] <= r[None, :]
    c[:, C_STRI:C_STRI + P] = r[:, None] < r[None, :]
    c[:, C_MASK:C_MASK + P] = np.where(r[None, :] <= r[:, None], 0, -BIG)
    pos = (r[:, None] + P * np.arange(TC)[None, :]).astype(np.float32)
    inv = (np.float32(10000.0) ** (-np.arange(0, ROPE, 2, dtype=np.float32) / np.float32(ROPE))).astype(np.float32)
    ang = pos[:, :, None] * inv[None, None, :]
    c[:, C_COS:C_COS + 64] = np.cos(ang).reshape(P, 64)
    c[:, C_SIN:C_SIN + 64] = np.sin(ang).reshape(P, 64)
    c[:, C_IOTA:C_IOTA + T] = np.arange(T)
    c[:, C_REV:C_REV + NE] = NE - np.arange(NE)
    c[:, C_ROW:C_ROW + NE] = T * np.arange(NE)
    c[:, C_EPS], c[:, C_EPS + 1] = EPS_LN, EPS_RMS
    return c


def kernel(**inputs):
    import numpy as np
    import concourse.bacc as bacc
    from concourse import mybir as mb
    from concourse.bass_utils import run_bass_kernel_spmd as run

    nc = bacc.Bacc("TRN2", target_bir_lowering=False, num_devices=1)
    arrays, aps = {}, {}
    for name in _NAMES + ["consts"]:
        v = np.ascontiguousarray(inputs[name]) if name != "consts" else constants()
        arrays["in_" + name] = v
        aps[name] = nc.dram_tensor("in_" + name, v.shape, mb.dt.from_np(v.dtype), kind="ExternalInput").ap()
    out = nc.dram_tensor("out", (1, T, D), mb.dt.float32, kind="ExternalOutput").ap()
    ybuf = nc.dram_tensor("expert_rows", (NE * T, D), mb.dt.float32, kind="Internal").ap()
    program(nc, aps, out, ybuf)
    return run(nc, [arrays], core_ids=[0]).results[0]["out"]
```
